# Optimizing a Trainium2 kernel written in Bass

```python
import math
import jax, jax.numpy as jnp
from jax import lax
import numpy as np

D_MODEL = 1024
BATCH = 1
SEQ = 256
DEPTH = 2

GRID_W = 64
CTX_LEN = 256
MIX_W = 512
IN_W = 5 * MIX_W
A_CONV = 3
B_GROUPS = 8
CHUNK = 128
C_CONV = 31
D_HEADS = 4
D_HEAD_DIM = 64
ROPE_THETA = 10000.0
N_ADA = 6
PEER_HEADS = 8
PEER_KEYS = 128
PEER_EXPERTS = PEER_KEYS * PEER_KEYS
PEER_QDIM = 256
PEER_TOPK = 16
PEER_BLOCK = 128
EPS = 1e-6
N_EVEN = (DEPTH + 1) // 2
N_ODD = DEPTH // 2

kernel_name = "hybrid_diffusion_conv_gmlp_conformer_diffattn_peer"

def rms_norm(x, g):
    xf = x.astype(jnp.float32)
    y = xf * lax.rsqrt(jnp.mean(xf * xf, axis=-1, keepdims=True) + EPS)
    return (y * g.astype(jnp.float32)).astype(x.dtype)

def modulate(h, shift, scale):
    return h * (1.0 + scale) + shift

def depthwise_conv(x, w):
    k = w.shape[0]
    return lax.conv_general_dilated(
        x, w[:, None, :].astype(x.dtype), window_strides=(1,),
        padding=((k // 2, k // 2),), dimension_numbers=('NWC', 'WIO', 'NWC'),
        feature_group_count=x.shape[-1])

def axial_rope_tables(rows):
    r = jnp.repeat(jnp.arange(rows, dtype=jnp.float32), GRID_W)
    col = jnp.tile(jnp.arange(GRID_W, dtype=jnp.float32), rows)
    n_freq = D_HEAD_DIM // 4
    inv = ROPE_THETA ** (-jnp.arange(n_freq, dtype=jnp.float32) / n_freq)
    ang = jnp.concatenate([r[:, None] * inv, col[:, None] * inv], axis=-1)
    return jnp.cos(ang), jnp.sin(ang)

def apply_rope(t, cos, sin):
    tf = t.astype(jnp.float32)
    t1, t2 = tf[..., 0::2], tf[..., 1::2]
    cs, sn = cos[None, :, None, None, :], sin[None, :, None, None, :]
    out = jnp.stack([t1 * cs - t2 * sn, t1 * sn + t2 * cs], axis=-1).reshape(t.shape)
    return out.astype(t.dtype)

def short_conv_mixer(hx, gate_c, gate_b, conv_w):
    return gate_b * depthwise_conv(gate_c * hx, conv_w)

def chunk_mlp_mixer(u, v, vnorm_g, w_s, b_s):
    bsz, L, _ = u.shape
    u = jax.nn.gelu(u)
    v = rms_norm(jax.nn.gelu(v), vnorm_g)
    v = v.reshape(bsz, L // CHUNK, CHUNK, B_GROUPS, MIX_W // B_GROUPS)
    s = jnp.einsum('gpq,bnqgc->bnpgc', w_s, v) + b_s.T[:, :, None]
    return u * s.reshape(bsz, L, MIX_W)

def even_mixer(h, w_in, w_out, conv_w, vnorm_g, w_s, b_s):
    a_h, a_c, a_b, b_u, b_v = jnp.split(h @ w_in, 5, axis=-1)
    ya = short_conv_mixer(a_h, a_c, a_b, conv_w)
    yb = chunk_mlp_mixer(b_u, b_v, vnorm_g, w_s, b_s)
    return jnp.concatenate([ya, yb], axis=-1) @ w_out

def conformer_conv(a, gate, conv_w, conv_b, norm_g):
    y = a * jax.nn.sigmoid(gate)
    y = depthwise_conv(y, conv_w) + conv_b
    return jax.nn.silu(rms_norm(y, norm_g))

def diff_attend(q, k, v, lam):
    s = jnp.einsum('bqhmd,bkhmd->bhmqk', q, k).astype(jnp.float32) * (D_HEAD_DIM ** -0.5)
    p = jax.nn.softmax(s, axis=-1)
    a = p[:, :, 0] - lam * p[:, :, 1]
    return jnp.einsum('bhqk,bkhe->bqhe', a.astype(v.dtype), v)

def diff_attend_blocked(q, k, v, lam):
    bsz, L = q.shape[:2]
    qb = q.reshape(bsz, L // CHUNK, CHUNK, *q.shape[2:]).swapaxes(0, 1)
    out = lax.map(lambda qi: diff_attend(qi, k, v, lam), qb)
    return out.swapaxes(0, 1).reshape(bsz, L, *out.shape[3:])

def odd_mixer(hx, hc, w_in, w_out, conv_w, conv_b, cnorm_g, qk_g, lam_p, subln_g,
              lam_init, cos, sin, need_ctx_out):
    bsz, L, _ = hx.shape

    def heads(t):
        return t.reshape(*t.shape[:2], D_HEADS, 2, D_HEAD_DIM)

    def values(t):
        return t.reshape(*t.shape[:2], D_HEADS, 2 * D_HEAD_DIM)

    lam_f = lam_p.astype(jnp.float32)
    lam = (jnp.exp(jnp.sum(lam_f[0] * lam_f[1])) - jnp.exp(jnp.sum(lam_f[2] * lam_f[3]))
           + lam_init)

    def finish(o):
        return (rms_norm(o, subln_g) * (1.0 - lam_init)).reshape(*o.shape[:2], MIX_W)

    ca, cg, qx, kx, vx = jnp.split(hx @ w_in, 5, axis=-1)
    qx = apply_rope(rms_norm(heads(qx), qk_g[0]), cos, sin)
    kx = apply_rope(rms_norm(heads(kx), qk_g[1]), cos, sin)
    if need_ctx_out:
        cca, ccg, qc, kc, vc = jnp.split(hc @ w_in, 5, axis=-1)
    else:
        kc, vc = jnp.split(hc @ w_in[:, 3 * MIX_W:], 2, axis=-1)
    kc = rms_norm(heads(kc), qk_g[1])
    vc = values(vc)
    k_all = jnp.concatenate([kc, kx], axis=1)
    v_all = jnp.concatenate([vc, values(vx)], axis=1)
    yx = jnp.concatenate([conformer_conv(ca, cg, conv_w, conv_b, cnorm_g),
                          finish(diff_attend_blocked(qx, k_all, v_all, lam))], axis=-1) @ w_out
    if not need_ctx_out:
        return yx, None
    qc = rms_norm(heads(qc), qk_g[0])
    yc = jnp.concatenate([conformer_conv(cca, ccg, conv_w, conv_b, cnorm_g),
                          finish(diff_attend(qc, kc, vc, lam))], axis=-1) @ w_out
    return yx, yc

def peer(h, wq, subkeys, u_tab, v_tab):
    shp = h.shape
    t = h.reshape(-1, D_MODEL)
    q = (t @ wq).reshape(-1, PEER_HEADS, 2, PEER_QDIM // 2)
    s = jnp.einsum('thpd,hpkd->thpk', q, subkeys).astype(jnp.float32)
    sv, si = lax.top_k(s, PEER_TOPK)
    cand = sv[:, :, 0, :, None] + sv[:, :, 1, None, :]
    cv, ci = lax.top_k(cand.reshape(*cand.shape[:2], PEER_TOPK * PEER_TOPK), PEER_TOPK)
    i1 = jnp.take_along_axis(si[:, :, 0], ci // PEER_TOPK, axis=-1)
    i2 = jnp.take_along_axis(si[:, :, 1], ci % PEER_TOPK, axis=-1)
    idx = i1 * PEER_KEYS + i2
    g = jax.nn.softmax(cv, axis=-1)
    nblk = t.shape[0] // PEER_BLOCK

    def block(args):
        tb, ib, gb = args
        act = jax.nn.gelu(jnp.einsum('td,thkd->thk', tb, u_tab[ib]).astype(jnp.float32))
        return jnp.einsum('thk,thkd->td', (gb * act).astype(tb.dtype), v_tab[ib])

    out = lax.map(block, (t.reshape(nblk, PEER_BLOCK, D_MODEL),
                          idx.reshape(nblk, PEER_BLOCK, PEER_HEADS, PEER_TOPK),
                          g.reshape(nblk, PEER_BLOCK, PEER_HEADS, PEER_TOPK)))
    return out.reshape(shp)

def setup_inputs(seed: int = 0) -> dict:
    key = jax.random.key(seed)
    ks = jax.random.split(key, 24)

    def nrm(k, shape, s):
        return jax.random.normal(k, shape, jnp.float32) * s

    return {
        "x": nrm(ks[0], (BATCH, SEQ, D_MODEL), 1.0),
        "c": nrm(ks[1], (BATCH, D_MODEL), 1.0),
        "ctx": nrm(ks[2], (BATCH, CTX_LEN, D_MODEL), 1.0),
        "c_ctx": nrm(ks[3], (D_MODEL,), 1.0),
        "w_ada": nrm(ks[4], (DEPTH, D_MODEL, N_ADA * D_MODEL), 0.5 * D_MODEL ** -0.5),
        "b_ada": nrm(ks[5], (DEPTH, N_ADA * D_MODEL), 0.01),
        "norm1_g": 1.0 + nrm(ks[6], (DEPTH, D_MODEL), 0.02),
        "norm2_g": 1.0 + nrm(ks[7], (DEPTH, D_MODEL), 0.02),
        "w_in": nrm(ks[8], (DEPTH, D_MODEL, IN_W), D_MODEL ** -0.5),
        "w_out": nrm(ks[9], (DEPTH, 2 * MIX_W, D_MODEL), (2 * MIX_W) ** -0.5),
        "a_conv_w": nrm(ks[10], (N_EVEN, A_CONV, MIX_W), A_CONV ** -0.5),
        "b_vnorm_g": 1.0 + nrm(ks[11], (N_EVEN, MIX_W), 0.02),
        "b_spatial_w": nrm(ks[12], (N_EVEN, B_GROUPS, CHUNK, CHUNK), 0.5 * CHUNK ** -0.5),
        "b_spatial_b": 1.0 + nrm(ks[13], (N_EVEN, B_GROUPS, CHUNK), 0.01),
        "c_conv_w": nrm(ks[14], (N_ODD, C_CONV, MIX_W), C_CONV ** -0.5),
        "c_conv_b": nrm(ks[15], (N_ODD, MIX_W), 0.01),
        "c_norm_g": 1.0 + nrm(ks[16], (N_ODD, MIX_W), 0.02),
        "d_qk_norm_g": 1.0 + nrm(ks[17], (N_ODD, 2, D_HEAD_DIM), 0.02),
        "d_lambda": nrm(ks[18], (N_ODD, 4, D_HEAD_DIM), 0.1),
        "d_subln_g": 1.0 + nrm(ks[19], (N_ODD, 2 * D_HEAD_DIM), 0.02),
        "peer_wq": nrm(ks[20], (DEPTH, D_MODEL, PEER_HEADS * PEER_QDIM), D_MODEL ** -0.5),
        "peer_subkeys": nrm(ks[21], (DEPTH, PEER_HEADS, 2, PEER_KEYS, PEER_QDIM // 2),
                            (PEER_QDIM // 2) ** -0.5),
        "peer_u": nrm(ks[22], (DEPTH, PEER_EXPERTS, D_MODEL), D_MODEL ** -0.5),
        "peer_v": nrm(ks[23], (DEPTH, PEER_EXPERTS, D_MODEL), 1.0),
    }

def reference(x, c, ctx, c_ctx, w_ada, b_ada, norm1_g, norm2_g, w_in, w_out,
              a_conv_w, b_vnorm_g, b_spatial_w, b_spatial_b,
              c_conv_w, c_conv_b, c_norm_g, d_qk_norm_g, d_lambda, d_subln_g,
              peer_wq, peer_subkeys, peer_u, peer_v):
    bsz, L, _ = x.shape
    rows = L // GRID_W
    cos, sin = axial_rope_tables(rows)
    for l in range(DEPTH):
        last = l == DEPTH - 1
        j = l // 2
        ada_x = (jax.nn.silu(c) @ w_ada[l] + b_ada[l]).reshape(bsz, 1, N_ADA, D_MODEL)
        hx = modulate(rms_norm(x, norm1_g[l]), ada_x[:, :, 0], ada_x[:, :, 1])
        ctx_read = (not last) or (l % 2 == 1)
        if ctx_read:
            ada_c = (jax.nn.silu(c_ctx) @ w_ada[l] + b_ada[l]).reshape(1, 1, N_ADA, D_MODEL)
            hc = modulate(rms_norm(ctx, norm1_g[l]), ada_c[:, :, 0], ada_c[:, :, 1])
        if l % 2 == 0:
            yx = even_mixer(hx, w_in[l], w_out[l], a_conv_w[j], b_vnorm_g[j],
                            b_spatial_w[j], b_spatial_b[j])
            yc = None if last else even_mixer(hc, w_in[l], w_out[l], a_conv_w[j], b_vnorm_g[j],
                                              b_spatial_w[j], b_spatial_b[j])
        else:
            lam_init = 0.8 - 0.6 * math.exp(-0.3 * l)
            yx, yc = odd_mixer(hx, hc, w_in[l], w_out[l], c_conv_w[j], c_conv_b[j], c_norm_g[j],
                               d_qk_norm_g[j], d_lambda[j], d_subln_g[j], lam_init, cos, sin,
                               not last)
        x = x + ada_x[:, :, 2] * yx
        h2 = modulate(rms_norm(x, norm2_g[l]), ada_x[:, :, 3], ada_x[:, :, 4])
        x = x + ada_x[:, :, 5] * peer(h2, peer_wq[l], peer_subkeys[l], peer_u[l], peer_v[l])
        if not last:
            ctx = ctx + ada_c[:, :, 2] * yc
            h2c = modulate(rms_norm(ctx, norm2_g[l]), ada_c[:, :, 3], ada_c[:, :, 4])
            ctx = ctx + ada_c[:, :, 5] * peer(h2c, peer_wq[l], peer_subkeys[l], peer_u[l], peer_v[l])
    return x


_drawn_inputs = setup_inputs


def setup_inputs(seed=0):
    import zlib

    import numpy as np

    out = dict(_drawn_inputs(seed))
    spreads = {}
    factors = {'b_vnorm_g': 4.483,
     'b_spatial_b': 3.936,
     'c_conv_b': 7.022,
     'c_norm_g': 7.487,
     'd_qk_norm_g': 6.451,
     'd_subln_g': 7.1}
    for name, (base, spread) in spreads.items():
        noise = np.random.default_rng([zlib.crc32(name.encode()), seed]).standard_normal(out[name].shape)
        drawn = base * np.exp(spread * noise) if base else spread * noise
        out[name] = __import__('jax').numpy.asarray(drawn.astype(out[name].dtype))
    for name, factor in factors.items():
        out[name] = (out[name] * factor).astype(out[name].dtype)
    return out
```

```python
import math
from contextlib import ExitStack

import numpy as np

import concourse.bass as bass
from concourse import mybir

F32 = mybir.dt.float32
U32 = mybir.dt.uint32
ALU = mybir.AluOpType
ACT = mybir.ActivationFunctionType
AX_X = mybir.AxisListType.X

P = 128
D = 1024
KC = D // P
TOK = 256
TT = TOK // P
MIX = 512
MC = MIX // P
GRID_W = 64
HEADS = 4
HD = 64
CONV_A = 3
CONV_C = 31
PAD_C = CONV_C // 2
N_ADA = 6
PH = 8
PK = 128
TOPK = 16
NSEL = PH * TOPK
EPS = 1e-6
LAM_INIT = 0.8 - 0.6 * math.exp(-0.3)
LOWEST = -3.4e38

BLK = 256
BLK_W = KC * BLK
SUB_W = 2 * PK
SLOT_W = BLK_W + SUB_W
WRING = 3
ADA_BLKS = N_ADA * D // BLK

RING = 8
BODY = RING
NBODY = NSEL // BODY
GRP = 2

PARTS = [("ident", P), ("iota", TOPK), ("cos", TT * 32), ("sin", TT * 32), ("c", KC * 2), ("b_ada", 2 * 48),
         ("norm_g", 2 * 2 * KC), ("a_conv", MC * CONV_A), ("c_conv", MC * CONV_C), ("c_conv_b", MC),
         ("c_norm_g", MC), ("vnorm_g", MIX), ("qk_g", 2 * HD), ("subln_g", P), ("lam", 4 * HD),
         ("b_spatial", MC * P)]
AT, W_CONST = {}, 0
for _name, _w in PARTS:
    AT[_name] = (W_CONST, W_CONST + _w)
    W_CONST += _w

WEIGHTS = {"v_rows": ("in", 8), "u_cols": ("in", 6), "ah_cols": ("in", 0), "ac_cols": ("in", 2), "ab_cols": ("in", 4),
           "cg_cols": ("in", 2), "ca_cols": ("in", 0), "q_rows": ("in", 4), "k_rows": ("in", 6), "x_rows": ("in", 8),
           "kc_rows": ("in", 6), "vc_rows": ("in", 8), "out_rows": ("out", 0), "query": ("wq", 0)}


def pairs(stage, *names):
    return [(name, stage, b) for name in names for b in range(2)]


def both(*step):
    return [(*step, t) for t in range(TT)]


def deal(steps, more):
    out = []
    for i, step in enumerate(steps):
        out += [step] + more[len(more) * i // len(steps):len(more) * (i + 1) // len(steps)]
    return out


def ada(layer, first, last):
    return [("ada", layer, b) for b in range(first, last)]


def project_even(stage):
    return (pairs(stage, "v_rows") + [("v_norm", stage)] + pairs(stage, "u_cols", "ah_cols", "ac_cols") + both("spatial", stage)
            + pairs(stage, "ab_cols"))


def project_out(stage):
    return [("out_rows", stage, b) for b in range(D // BLK)]


def first_heads(stage):
    return [("query", stage, 0), ("query", stage, 1), ("search", stage, 0), ("query", stage, 2)]


def next_head(stage, h):
    return [("search", stage, h)] + ([("query", stage, h + 2)] if h < PH - 1 else [])


SHARE = {"ada": 1, "query": 4, "spatial": 1, "norm": 1, "norm_ctx": 1, "mods": 0, "gate": 1, "v_norm": 1, "turn_back": 1,
         "lam": 1}


def schedule():
    before = {
        0: ada(0, 0, 8) + [("mods", 0, 0)] + both("norm", 0, 0) + deal(project_even(0), ada(0, 8, 18)) + [("gate", 0, 0)]
        + deal(project_out(0), ada(0, 18, 22)) + [("mods", 0, 1)] + both("norm", 0, 1)
        + deal(both("turn_back", 0), ada(0, 22, 24)) + first_heads(0) + [("gate", 0, 1)],
        1: [],
        2: both("norm", 2, 0) + pairs(2, "cg_cols", "ca_cols") + [("conv", 2)] + pairs(2, "k_rows", "q_rows", "x_rows")
        + [("qk_norm", 2), ("qk_turn", 2)] + [("attend", 2, i) for i in range(TT * HEADS + 1)] + [("conv_norm", 2)]
        + both("o_norm", 2) + project_out(2) + both("norm", 2, 1) + both("turn_back", 2) + first_heads(2),
    }
    during = {
        0: [("mods", 1, 0), ("gate", 1, 0)] + both("norm", 1, 0) + project_even(1) + project_out(1)
        + [("mods", 1, 1)] + both("norm", 1, 1) + both("turn_back", 1) + [("gate", 1, 1)] + first_heads(1),
        1: ada(1, 0, ADA_BLKS) + [("mods", 2, 2)] + both("norm_ctx", 2) + pairs(2, "kc_rows", "vc_rows")
        + [("ctx_keys", 2), ("lam", 2), ("mods", 2, 0), ("gate", 2, 0), ("mods", 2, 1), ("gate", 2, 1)],
        2: [],
    }
    program = []
    for stage in range(3):
        program += [("step", step) for step in before[stage]]
        own = [next_head(stage, h) for h in range(1, PH)]
        gaps = own + [[] for _ in range(TT * NBODY - len(own))]
        free = len(gaps) - 1 - len(own)
        total, spent = sum(SHARE.get(step[0], 2) for step in during[stage]), 0
        for step in during[stage]:
            gaps[len(own) + spent * free // (total + 1)].append(step)
            spent += SHARE.get(step[0], 2)
        for t in range(TT):
            T = stage * TT + t
            program.append(("open", T))
            h = 0
            while h < NBODY:
                k = 1
                while h + k < NBODY and not gaps[t * NBODY + h + k - 1]:
                    k += 1
                program.append(("bodies", T, h, k))
                h += k
                last = gaps[t * NBODY + h - 1]
                if h < NBODY:
                    program += [("step", step) for step in last]
            program.append(("close", T))
            program += [("step", step) for step in last]
    return program


def weight_blocks(program):
    order = []
    for item in program:
        if item[0] != "step":
            continue
        name, *args = item[1]
        if name == "ada":
            order.append(("ada", args[0], args[1]))
        elif name in WEIGHTS and not (name == "query" and args[1] == PH):
            kind, first = WEIGHTS[name]
            order.append((kind, args[0] // 2, first + args[1]))
    return order


def build(nc, A):
    with ExitStack() as ctx:
        def sb(name, shape, dt=F32):
            return ctx.enter_context(nc.sbuf_tensor(name, shape, dt))

        def sem(name):
            return ctx.enter_context(nc.semaphore(name))

        const = sb("const", [P, W_CONST])
        wst = sb("wst", [P, 8 * P])
        ones = sb("ones", [P, P])
        zeros = sb("zeros", [P, 512], mybir.dt.bfloat16)
        x = sb("x", [P, 2 * TT, D])
        silu_c = sb("silu_c", [P, KC, 2])
        ada_c = sb("ada_c", [P, 48, 2])
        modg = sb("modg", [P, 3, KC])
        gate_mix = sb("gate_mix", [P, D])
        gate_peer = sb("gate_peer", [P, 2, D])
        gdiag = sb("gdiag", [P, 4, P])
        wring = sb("wring", [P, WRING, SLOT_W])
        hT = sb("hT", [P, KC, TOK])
        h2 = sb("h2", [P, 2, TT, D])
        stat = sb("stat", [P, 64])
        sp_t = sb("sp_t", [P, P])
        ss_heads, ms_heads, root_heads = (sb(s, [P, 32]) for s in ("ss_heads", "ms_heads", "root_heads"))
        smax, nmax, psums, prec = (sb(s, [P, 2, 2]) for s in ("smax", "nmax", "psums", "prec"))
        uv = sb("uv", [P, RING, 2 * D])
        diag = sb("diag", [P, RING, P])
        idx = sb("idx", [P, 2, TT, NSEL], U32)
        gw = sb("gw", [P, 2, TT, NSEL])
        stage_idx = sb("stage_idx", [P, 2, RING], U32)
        dots = sb("dots", [P, BODY])
        gel = sb("gel", [P, BODY])
        work = sb("work", [P, 8704])

        def view(base, off, *shape):
            n = int(np.prod(shape))
            flat = base[:, off:off + n]
            if len(shape) == 1:
                return flat
            if len(shape) == 2:
                return flat.rearrange("p (a b) -> p a b", a=shape[0])
            return flat.rearrange("p (a b c) -> p a b c", a=shape[0], b=shape[1])

        def C(name, *shape):
            a, b = AT[name]
            return view(const, a, *shape) if shape else const[:, a:b]

        xn = view(work, 0, 2, D)
        v_rows = view(work, 2048, TT, MIX)
        uT = view(work, 3072, MC, TOK)
        ahT = view(work, 4096, MC, TOK)
        apT = view(work, 5120, MC, TOK + 2)
        acT = view(work, 4096, MC, TOK)
        yT = view(work, 6656, 2 * MC, TOK)
        hcT = view(work, 6656, KC, TOK)
        kvc = view(work, 2048, 4, MIX)
        kcT = view(work, 4096, HEADS, TOK)
        sqc = view(work, 5248, 2, MIX)
        orow = view(work, 5248, TT, MIX)
        ring = uv[:, :, :].rearrange("p a b -> p (a b)")
        qk = view(ring, 0, 4, MIX)
        vx = view(ring, 2048, TT, MIX)
        sgT = view(ring, 3072, MC, TOK)
        cpT = view(ring, 4096, MC, TOK + 2 * PAD_C)
        ccT = view(ring, 5248, MC, TOK)
        sq = view(ring, 6272, 4, MIX)
        qT = view(ring, 8320, HEADS, TOK)
        kxT = view(ring, 9344, HEADS, TOK)
        prob = view(ring, 10368, 2, 2, MIX)
        pT = view(ring, 12416, 2, MIX)
        csq = view(ring, 13440, MC, TOK)
        rr_ms, rr_root = view(ring, 14464, TOK), view(ring, 14720, TOK)
        qh = view(work, 2048, 2, 2, TOK)
        sc = view(work, 3072, 2, 2 * TT, PK)
        sc_rest = view(work, 4096, 2 * TT, PK)
        cand = view(work, 4608, TT, TOPK, TOPK)
        cand_rest = view(work, 5120, TT, NSEL * 2)
        sv = view(work, 5632, 2 * TT * TOPK)
        cv = view(work, 5696, TT, TOPK)
        e16 = view(work, 5728, TT, TOPK)
        e_stat = view(work, 5760, 2, TT)
        side = view(work, 5764, 2 * TT, TOPK)
        pos_f = view(work, 5828, 2 * TT, TOPK)
        side_no = view(work, 5892, 2 * TT, TOPK)
        hot = view(work, 6656, 2 * TT, TOPK, TOPK)
        si = sb("si", [P, 2 * TT, TOPK], U32)
        ci = sb("ci", [P, TT, TOPK], U32)
        pick = sb("pick", [P, 2 * TT, TOPK], U32)

        psum = ctx.enter_context(nc.psum_tensor("psum", [P, 8, 512], F32))
        acc = psum[:, 0:2, :]

        loaded = sem("loaded")
        constants_set = sem("constants_set")
        w_landed = [sem(f"w_landed{i}") for i in range(WRING)]
        act_bank_full, act_took = sem("act_bank_full"), sem("act_took")
        dve_bank_full, dve_took = sem("dve_bank_full"), sem("dve_took")
        dve_chain = sem("dve_chain")
        silu_ready = sem("silu_ready")
        mods_ready = sem("mods_ready")
        gdiag_ready = sem("gdiag_ready")
        ms_ready, root_ready = sem("ms_ready"), sem("root_ready")
        xn_ready = sem("xn_ready")
        v_ready = sem("v_ready")
        sc_used = sem("sc_used")
        cv_ready, exp_ready = sem("cv_ready"), sem("exp_ready")
        idx_ready = sem("idx_ready")
        lam_sums, lam_exps = sem("lam_sums"), sem("lam_exps")
        kc_normed, roped = sem("kc_normed"), sem("roped")
        nmax_ready, prob_ready, mixed_ready = sem("nmax_ready"), sem("prob_ready"), sem("mixed_ready")
        cc_ready, csq_ready, cn_ready, conv_out = sem("cc_ready"), sem("csq_ready"), sem("cn_ready"), sem("conv_out")
        on_ready = sem("on_ready")
        staged, slot_claimed = sem("staged"), sem("slot_claimed")
        uv_landed = [sem(f"uv_landed{i}") for i in range(RING)]
        dots_ready, gelu_ready, diag_ready = sem("dots_ready"), sem("gelu_ready"), sem("diag_ready")
        uv_used = sem("uv_used")
        acc_ready, acc_free = sem("acc_ready"), sem("acc_free")
        x_rows_ready, out_stored = sem("x_rows_ready"), sem("out_stored")

        N_LOADS = 2 + 2 * TT
        program = schedule()
        blocks = weight_blocks(program)
        taken = {}
        multiplied = []
        block = ctx.enter_context(nc.Block())

        class Tally(dict):

            def up(self, what, by=1):
                self[what] = self.get(what, 0) + by
                return self[what]

        class Banks:

            def __init__(self, first, full, took):
                self.first, self.full, self.took, self.n = first, full, took, 0

            def bank(self):
                return psum[:, self.first + self.n % 3, :]

            def open(self, pe):
                if self.n >= 3:
                    pe.wait_ge(self.took, self.n - 2)
                return self.bank()

            def fill(self, last):
                last.then_inc(self.full, 1)
                self.n += 1

            def full_bank(self, reader):
                reader.wait_ge(self.full, self.n + 1)
                return self.bank()

            def emptied(self, last):
                last.then_inc(self.took, 1)
                self.n += 1

        def act_banks():
            return Banks(2, act_bank_full, act_took)

        def dve_banks():
            return Banks(5, dve_bank_full, dve_took)

        def shift(stage, which):
            j = 3 if which == 1 else 0
            return ada_c[:, j * KC:(j + 1) * KC, 1 if stage == 0 or which == 2 else 0]

        def walk(steps, open_tile, bodies, close_tile):
            for kind, what, *more in program:
                if kind == "step":
                    if what[0] in steps:
                        steps[what[0]](*what[1:])
                elif kind == "open":
                    open_tile(what)
                elif kind == "close":
                    close_tile(what)
                else:
                    bodies(what, *more)

        @block.tensor
        def _(pe):
            n = Tally()
            to_act, to_dve = act_banks(), dve_banks()
            mm, turn = nc.tensor.matmul, nc.tensor.transpose
            ident = C("ident")

            def weights():
                k = n.up("block") - 1
                pe.wait_ge(w_landed[k % WRING], 16 * (k // WRING + 1))
                return wring[:, k % WRING, :]

            def kc(w):
                return w[:, 0:BLK_W].rearrange("p (k c) -> p k c", k=KC)

            def block_done(banks):
                multiplied.append((banks.full, banks.n))

            def ada_blk(layer, b):
                if layer == 0 and b == 0:
                    pe.wait_ge(silu_ready, 1)
                w = kc(weights())
                bank = to_dve.open(pe)
                for i in range(2):
                    for k in range(KC):
                        last = mm(bank[:, 2 * i:2 * i + 2], w[:, k, i * P:(i + 1) * P], silu_c[:, k, :],
                                  start=(k == 0), stop=(k == KC - 1))
                to_dve.fill(last)
                block_done(to_dve)

            def gate(stage, which):
                for half in range(2):
                    pe.wait_ge(gdiag_ready, n.up("gdiag_ready"))
                    bank = to_act.open(pe)
                    for i in range(4):
                        last = mm(bank[:, i * P:(i + 1) * P], ones[:, :], gdiag[:, i, :], start=True, stop=True)
                    to_act.fill(last)
                    taken["gdiag", n["gdiag_ready"]] = (act_bank_full, to_act.n)
                taken["gate", stage, which] = (act_took, to_act.n)

            def turn_rows():
                k = n.up("xn_ready")
                pe.wait_ge(xn_ready, k)
                row = xn[:, (k - 1) % 2, :]
                for half, banks in ((0, to_act), (1, to_dve)):
                    bank = banks.open(pe)
                    for i in range(4):
                        c = half * 4 + i
                        last = turn(bank[:, i * P:(i + 1) * P], row[:, c * P:(c + 1) * P], ident)
                    banks.fill(last)
                n["hT"] = (to_act.n, to_dve.n)

            def norm(stage, which, t):
                turn_rows()

            def norm_ctx(stage, t):
                turn_rows()

            def wait_hT():
                pe.wait_ge(act_took, n["hT"][0])
                pe.wait_ge(dve_took, n["hT"][1])

            def token_major(banks, srcs):
                w = kc(weights())
                for src, t in srcs:
                    bank = banks.open(pe)
                    for k in range(KC):
                        last = mm(bank[:, 0:BLK], src[:, k, t * P:(t + 1) * P], w[:, k, :], start=(k == 0), stop=(k == KC - 1))
                    banks.fill(last)
                block_done(banks)

            def channel_major(banks):
                wait_hT()
                w = kc(weights())
                for i in range(2):
                    bank = banks.open(pe)
                    for k in range(KC):
                        last = mm(bank[:, 0:TOK], w[:, k, i * P:(i + 1) * P], hT[:, k, :], start=(k == 0), stop=(k == KC - 1))
                    banks.fill(last)
                block_done(banks)

            def v_project(stage, b):
                wait_hT()
                token_major(to_act, [(hT, t) for t in range(TT)])
                taken["v", n.up("v")] = (act_took, to_act.n)

            def noted(what):
                channel_major(to_act)
                taken[what, n.up(what)] = (act_took, to_act.n)

            def spatial(stage, t):
                pe.wait_ge(v_ready, n.up("v_ready"))
                for j in range(MC):
                    bank = to_dve.open(pe)
                    to_dve.fill(mm(bank[:, 0:2 * P], v_rows[:, t, j * P:(j + 1) * P], wst[:, j * 2 * P:(j + 1) * 2 * P],
                                   start=True, stop=True))

            def rows(src):
                wait_hT()
                token_major(to_act, [(src, t) for t in range(TT)])
                taken["rows"] = (act_took, to_act.n)

            def turn_heads(tiles):
                for tile in tiles:
                    bank = to_act.open(pe)
                    for h in range(HEADS):
                        last = turn(bank[:, h * P:(h + 1) * P], tile[:, h * P:(h + 1) * P], ident)
                    to_act.fill(last)

            def ctx_keys(stage):
                taken["ctx rows"] = (act_took, to_act.n)
                pe.wait_ge(kc_normed, 1)
                turn_heads([kvc[:, i, :] for i in range(2)])

            def qk_turn(stage):
                pe.wait_ge(roped, 1)
                turn_heads([qk[:, i, :] for i in range(4)])
                n["qkT"] = to_act.n

            def attend(stage, i):
                if i == 0:
                    pe.wait_ge(act_took, n["qkT"])
                if i < TT * HEADS:
                    t, h = i // HEADS, i % HEADS
                    taken["scores of", i] = (dve_bank_full, to_dve.n)
                    for m in range(2):
                        half = slice(m * HD, (m + 1) * HD)
                        bank = to_dve.open(pe)
                        for k, keys in enumerate((kxT, kcT)):
                            last = mm(bank[:, k * TOK:(k + 1) * TOK], qT[half, h, t * P:(t + 1) * P], keys[half, h, :],
                                      start=True, stop=True)
                        to_dve.fill(last)
                if i > 0:
                    h = (i - 1) % HEADS
                    pe.wait_ge(mixed_ready, i)
                    bank = to_act.open(pe)
                    for k in range(4):
                        last = turn(bank[:, k * P:(k + 1) * P], prob[:, (i - 1) % 2, 0, k * P:(k + 1) * P], ident)
                    to_act.fill(last)
                    pe.wait_ge(act_took, to_act.n)
                    bank = to_dve.open(pe)
                    for k, values in enumerate((vx[:, 0, :], vx[:, 1, :], kvc[:, 2, :], kvc[:, 3, :])):
                        last = mm(bank[:, 0:P], pT[:, (i - 1) % 2, k * P:(k + 1) * P], values[:, h * P:(h + 1) * P],
                                  start=(k == 0), stop=(k == 3))
                    to_dve.fill(last)

            def conv_norm(stage):
                pe.wait_ge(csq_ready, 1)
                bank = to_dve.open(pe)
                for j in range(MC):
                    last = mm(bank[:, 0:TOK], ones[:, :], csq[:, j, :], start=(j == 0), stop=(j == MC - 1))
                to_dve.fill(last)

            def o_norm(stage, t):
                pe.wait_ge(on_ready, t + 1)
                bank = to_act.open(pe)
                for h in range(HEADS):
                    last = turn(bank[:, h * P:(h + 1) * P], orow[:, t, h * P:(h + 1) * P], ident)
                to_act.fill(last)

            def out_rows(stage, b):
                if b == 0 and stage < 2:
                    pe.wait_ge(dve_took, to_dve.n)
                elif b == 0:
                    pe.wait_ge(act_took, to_act.n)
                    pe.wait_ge(conv_out, 1)
                token_major(to_dve, [(yT, t) for t in range(TT)])

            def turn_back(stage, t):
                wait_hT()
                for half in range(2):
                    bank = to_act.open(pe)
                    for i in range(4):
                        last = turn(bank[:, i * P:(i + 1) * P], hT[:, half * 4 + i, t * P:(t + 1) * P], ident)
                    to_act.fill(last)
                taken["h2", stage, t] = (act_took, to_act.n)

            def query(stage, h):
                if h > 0:
                    pe.wait_ge(act_took, n["qh"])
                    bank = to_act.open(pe)
                    for q in range(2):
                        for t in range(TT):
                            o = (q * TT + t) * P
                            last = mm(bank[:, o:o + P], qh[:, (h - 1) % 2, q, t * P:(t + 1) * P],
                                      n["wq"][:, BLK_W + q * PK:BLK_W + (q + 1) * PK], start=True, stop=True)
                    to_act.fill(last)
                    block_done(to_act)
                    taken["scores", n.up("scores")] = (act_took, to_act.n)
                if h < PH:
                    wait_hT()
                    n["wq"] = weights()
                    w = kc(n["wq"])
                    for q in range(2):
                        bank = to_act.open(pe)
                        for k in range(KC):
                            last = mm(bank[:, 0:TOK], w[:, k, q * P:(q + 1) * P], hT[:, k, :],
                                      start=(k == 0), stop=(k == KC - 1))
                        to_act.fill(last)
                    n["qh"] = to_act.n

            steps = {"ada": ada_blk, "gate": gate, "norm": norm, "norm_ctx": norm_ctx, "v_rows": v_project,
                     "u_cols": lambda stage, b: noted("u"), "ah_cols": lambda stage, b: noted("ah"),
                     "ac_cols": lambda stage, b: channel_major(to_dve), "ab_cols": lambda stage, b: channel_major(to_dve),
                     "spatial": spatial, "cg_cols": lambda stage, b: noted("cg"),
                     "ca_cols": lambda stage, b: channel_major(to_dve),
                     "q_rows": lambda stage, b: rows(hT), "k_rows": lambda stage, b: rows(hT), "x_rows": lambda stage, b: rows(hT),
                     "kc_rows": lambda stage, b: rows(hcT), "vc_rows": lambda stage, b: rows(hcT),
                     "ctx_keys": ctx_keys, "qk_turn": qk_turn, "attend": attend, "conv_norm": conv_norm, "o_norm": o_norm,
                     "out_rows": out_rows, "turn_back": turn_back, "query": query}

            def open_tile(T):
                if T:
                    pe.wait_ge(acc_free, T)
                for b in range(2):
                    mm(acc[:, b, :], zeros[:, 0:P], zeros[:, :], start=True, stop=False)

            def add_values(T, it):
                for c in range(BODY):
                    pe.wait_ge(diag_ready, it * BODY + (T * NSEL + c + 1))
                    for b in range(2):
                        last = mm(acc[:, b, :], diag[:, c % RING, :], uv[:, c % RING, D + 512 * b:D + 512 * (b + 1)],
                                  start=False, stop=False)
                    last.then_inc(uv_used, 1)

            def bodies(T, first, count):
                if count == 1:
                    add_values(T, first)
                    return
                with pe.Fori(first, first + count) as it:
                    add_values(T, it)

            def close_tile(T):
                for b in range(2):
                    last = mm(acc[:, b, :], zeros[:, 0:P], zeros[:, :], start=False, stop=True)
                last.then_inc(acc_ready, 1)

            pe.sem_inc(uv_used, RING)
            pe.wait_ge(constants_set, 2)
            pe.wait_ge(loaded, 16 * N_LOADS)
            walk(steps, open_tile, bodies, close_tile)

        @block.sync
        def _(sp):
            for dst, src in ((const[:, :], A["const"]), (wst[:, :], A["wst"])):
                sp.dma_start(dst, src).then_inc(loaded, 16)
            for i in range(2 * TT):
                sp.dma_start(x[:, i, :], A["xin"][i]).then_inc(loaded, 16)
            for n, (kind, layer, b) in enumerate(blocks):
                if n >= WRING:
                    sp.wait_ge(*multiplied[n - WRING])
                wide = SLOT_W if kind == "wq" else BLK_W
                sp.dma_start(wring[:, n % WRING, 0:wide], A[{"out": "out_w"}.get(kind, kind)][layer, b]).then_inc(w_landed[n % WRING], 16)
            for t in range(TT):
                sp.wait_ge(x_rows_ready, t + 1)
                sp.dma_start(A["result"][t], x[:, TT + t, :]).then_inc(out_stored, 16)
            sp.wait_ge(out_stored, 16 * TT)

        @block.gpsimd
        def _(pool):
            tables = [A["uv0"], A["uv1"]]

            def gathers(T, it):
                stage, t = T // TT, T % TT
                pool.wait_ge(idx_ready, it + (stage * PH + 1))
                pool.sem_inc(slot_claimed, 1)
                for half in range(2):
                    nc.gpsimd.tensor_copy(stage_idx[:, half, :],
                                          idx[:, stage % 2, t, bass.ds(it * TOPK + half * RING, RING)]).then_inc(staged, 1)
                    pool.wait_ge(staged, it * 2 + (T * PH * 2 + half + 1))
                    for s in range(RING):
                        pool.wait_ge(uv_used, it * TOPK + (T * NSEL + half * RING + s + 1))
                        pool.sem_inc(slot_claimed, 1)
                        nc.gpsimd.indirect_dma_start(
                            out=uv[:, s, :], out_offset=None, in_=tables[stage // 2],
                            in_offset=bass.IndirectOffsetOnAxis(ap=stage_idx[:, half, s:s + 1], axis=0),
                        ).then_inc(uv_landed[s], 16)

            for T in range(3 * TT):
                with pool.Fori(0, PH) as it:
                    gathers(T, it)

        @block.scalar
        def _(act):
            n = Tally()
            mine = act_banks()
            f = nc.scalar.activation

            def empty(dst, width, func=ACT.Copy, a=None, **kw):
                src = mine.full_bank(act)[:, 0:width]
                if a:
                    src = src.rearrange("p (a b) -> p a b", a=a)
                mine.emptied(f(dst, src, func, **kw))

            def root(dst, src):
                act.wait_ge(ms_ready, n.up("ms_ready"))
                f(dst, src, ACT.Sqrt).then_inc(root_ready, 1)

            def gate(stage, which):
                dst = gate_peer[:, stage % 2, :] if which else gate_mix
                for half in range(2):
                    empty(dst[:, half * 512:(half + 1) * 512], 512)

            def modulate(dst, t, stage, which):
                act.wait_ge(mods_ready, n["mods"])
                bank = mine.full_bank(act)
                for i in range(4):
                    last = f(dst[:, i, t * P:(t + 1) * P], bank[:, i * P:(i + 1) * P], ACT.Identity,
                             scale=modg[:, which, i:i + 1], bias=shift(stage, which)[:, i:i + 1])
                mine.emptied(last)

            def norm(stage, which, t):
                k = n.up("xn")
                root(stat[:, 4 + (k - 1) % 2:5 + (k - 1) % 2], stat[:, 2 + (k - 1) % 2:3 + (k - 1) % 2])
                modulate(hT, t, stage, which)

            def norm_ctx(stage, t):
                k = n.up("xn")
                root(stat[:, 4 + (k - 1) % 2:5 + (k - 1) % 2], stat[:, 2 + (k - 1) % 2:3 + (k - 1) % 2])
                modulate(hcT, t, 2, 2)

            def v_project(stage, b):
                for t in range(TT):
                    empty(v_rows[:, t, b * BLK:(b + 1) * BLK], BLK, ACT.Gelu_apprx_tanh)

            def v_norm(stage):
                root(stat[:, 10:12], stat[:, 8:10])

            def channels(dst, b, func):
                for i in range(2):
                    empty(dst[:, 2 * b + i, :], TOK, func)

            def rows(dst, b):
                for t in range(TT):
                    empty(dst[:, t, b * BLK:(b + 1) * BLK], BLK)

            def lam(stage):
                act.wait_ge(lam_sums, 1)
                f(stat[:, 14:16], stat[:, 12:14], ACT.Exp).then_inc(lam_exps, 1)

            def ctx_keys(stage):
                root(root_heads[:, 0:16], ms_heads[:, 0:16])
                for t in range(TT):
                    empty(kcT[:, :, t * P:(t + 1) * P], 4 * P, a=HEADS)

            def qk_norm(stage):
                root(root_heads[:, :], ms_heads[:, :])

            def qk_turn(stage):
                for dst in (qT, kxT):
                    for t in range(TT):
                        empty(dst[:, :, t * P:(t + 1) * P], 4 * P, a=HEADS)

            def attend(stage, i):
                if i < TT * HEADS:
                    act.wait_ge(nmax_ready, i + 1)
                    for m in range(2):
                        bank = psum[:, 5 + (taken["scores of", i][1] + m) % 3, :]
                        last = f(prob[:, i % 2, m, :], bank, ACT.Exp, scale=HD ** -0.5,
                                 bias=nmax[:, i % 2, m:m + 1], accum_out=psums[:, i % 2, m:m + 1])
                    last.then_inc(prob_ready, 1)
                if i > 0:
                    empty(pT[:, (i - 1) % 2, :], 4 * P)

            def conv_norm(stage):
                act.wait_ge(cc_ready, 1)
                f(csq[:, :, :], ccT[:, :, :], ACT.Square).then_inc(csq_ready, 1)
                root(rr_root[:, :], rr_ms[:, :])
                act.wait_ge(cn_ready, 1)
                for j in range(MC):
                    last = f(yT[:, j, :], ccT[:, j, :], ACT.Silu, scale=C("c_norm_g")[:, j:j + 1])
                last.then_inc(conv_out, 1)

            def o_norm(stage, t):
                root(stat[:, 20:24], stat[:, 16:20])
                empty(yT[:, MC:, t * P:(t + 1) * P], 4 * P, a=HEADS)

            def turn_back(stage, t):
                for half in range(2):
                    empty(h2[:, stage % 2, t, half * 512:(half + 1) * 512], 512)

            def query(stage, h):
                if h > 0:
                    k = n.up("scores")
                    if k > 2:
                        act.wait_ge(sc_used, k - 2)
                    empty(sc[:, (k - 1) % 2, :, :], 4 * P, a=4)
                if h < PH:
                    for q in range(2):
                        empty(qh[:, h % 2, q, :], TOK)

            def search(stage, h):
                act.wait_ge(cv_ready, n.up("cv"))
                f(e16[:, :, :], e16[:, :, :], ACT.Exp).then_inc(exp_ready, 1)

            def mods(stage, which):
                n.up("mods")

            steps = {"mods": mods, "gate": gate, "norm": norm, "norm_ctx": norm_ctx, "v_rows": v_project, "v_norm": v_norm,
                     "u_cols": lambda stage, b: channels(uT, b, ACT.Gelu_apprx_tanh),
                     "ah_cols": lambda stage, b: channels(ahT, b, ACT.Copy),
                     "cg_cols": lambda stage, b: channels(sgT, b, ACT.Sigmoid),
                     "q_rows": lambda stage, b: rows(qk[:, 0:2, :], b), "k_rows": lambda stage, b: rows(qk[:, 2:4, :], b),
                     "x_rows": lambda stage, b: rows(vx, b), "kc_rows": lambda stage, b: rows(kvc[:, 0:2, :], b),
                     "vc_rows": lambda stage, b: rows(kvc[:, 2:4, :], b), "ctx_keys": ctx_keys, "lam": lam,
                     "qk_norm": qk_norm, "qk_turn": qk_turn, "attend": attend, "conv_norm": conv_norm, "o_norm": o_norm,
                     "turn_back": turn_back, "query": query, "search": search}

            def gelus(T, it):
                for c in range(0, BODY, GRP):
                    act.wait_ge(dots_ready, it * BODY + (T * NSEL + c + GRP))
                    f(gel[:, c:c + GRP], dots[:, c:c + GRP], ACT.Gelu_apprx_tanh).then_inc(gelu_ready, 1)

            def bodies(T, first, count):
                if count == 1:
                    gelus(T, first)
                    return
                with act.Fori(first, first + count) as it:
                    gelus(T, it)

            act.wait_ge(loaded, 16 * N_LOADS)
            f(silu_c[:, :, :], C("c", KC, 2), ACT.Silu).then_inc(silu_ready, 1)
            walk(steps, lambda T: None, bodies, lambda T: None)

        @block.vector
        def _(dve):
            n = Tally()
            mine = dve_banks()
            v = nc.vector
            chain = [0]

            def link(*instructions):
                for ins in instructions:
                    ins.then_inc(dve_chain, 1)
                chain[0] += len(instructions)
                dve.wait_ge(dve_chain, chain[0])

            def emptied(ins):
                mine.emptied(ins)
                dve.wait_ge(dve_took, mine.n)

            def mean_root(dst, ms, ss, count):
                v.tensor_scalar(ms, ss, 1.0 / count, EPS, ALU.mult, ALU.add).then_inc(ms_ready, 1)
                dve.wait_ge(root_ready, n.up("root"))
                link(v.reciprocal(dst, dst))

            def ada_blk(layer, b):
                bank = mine.full_bank(dve)[:, 0:4].rearrange("p (a b) -> p a b", a=2)
                bias = C("b_ada")[:, layer * 48 + 2 * b:layer * 48 + 2 * b + 2]
                emptied(v.tensor_tensor(ada_c[:, 2 * b:2 * b + 2, :], bank, bias.unsqueeze(2).to_broadcast([P, 2, 2]), ALU.add))

            def mods(stage, which):
                j = 4 if which == 1 else 1
                own = 1 if stage == 0 or which == 2 else 0
                v.scalar_tensor_tensor(out=modg[:, which, :], in0=ada_c[:, j * KC:(j + 1) * KC, own], scalar=1.0,
                                       in1=C("norm_g", 4, KC)[:, 2 * (stage // 2) + which % 2, :],
                                       op0=ALU.add, op1=ALU.mult).then_inc(mods_ready, 1)
                dve.wait_ge(mods_ready, n.up("mods"))

            def gate(stage, which):
                s = 0 if stage else 1
                j = 5 if which else 2
                for half in range(2):
                    k = n.up("gdiag")
                    if k > 1:
                        dve.wait_ge(*taken["gdiag", k - 1])
                    for i in range(4):
                        c = j * KC + half * 4 + i
                        last = v.tensor_scalar(gdiag[:, i, :], C("ident"), ada_c[:, c, s:s + 1], None, ALU.mult)
                    last.then_inc(gdiag_ready, 1)

            def norm_rows(tile, dst, dst_t, stage, which):
                k = n.up("xn")
                p = (k - 1) % 2
                ss, ms, r = (stat[:, i + p:i + p + 1] for i in (0, 2, 4))
                row = x[:, tile, :]
                link(v.tensor_tensor_reduce(out=xn[:, p, :], in0=row, in1=row, scale=1.0, scalar=0.0,
                                            op0=ALU.mult, op1=ALU.add, accum_out=ss))
                mean_root(r, ms, ss, D)
                v.tensor_scalar(xn[:, p, :], row, r, None, ALU.mult).then_inc(xn_ready, 1)
                bank = mine.full_bank(dve)
                for i in range(4):
                    last = v.tensor_scalar(dst[:, 4 + i, dst_t * P:(dst_t + 1) * P], bank[:, i * P:(i + 1) * P],
                                           modg[:, which, 4 + i:5 + i], shift(stage, which)[:, 4 + i:5 + i], ALU.mult, ALU.add)
                emptied(last)

            def norm(stage, which, t):
                norm_rows((TT if stage else 0) + t, hT, t, stage, which)

            def norm_ctx(stage, t):
                norm_rows(t, hcT, t, 2, 2)

            def v_norm(stage):
                dve.wait_ge(*taken["v", n.up("v", 2)])
                link(*[v.tensor_tensor_reduce(out=yT[:, 2 * t:2 * t + 2, :].rearrange("p a b -> p (a b)"), in0=v_rows[:, t, :],
                                              in1=v_rows[:, t, :], scale=1.0, scalar=0.0, op0=ALU.mult, op1=ALU.add,
                                              accum_out=stat[:, 6 + t:7 + t]) for t in range(TT)])
                mean_root(stat[:, 10:12], stat[:, 8:10], stat[:, 6:8], MIX)
                for t in range(TT):
                    v.scalar_tensor_tensor(out=v_rows[:, t, :], in0=v_rows[:, t, :], scalar=stat[:, 10 + t:11 + t],
                                           in1=C("vnorm_g"), op0=ALU.mult, op1=ALU.mult).then_inc(v_ready, 1)
                link(v.memset(apT[:, :, 0:1], 0.0), v.memset(apT[:, :, TOK + 1:TOK + 2], 0.0))

            def ac_cols(stage, b):
                w = C("a_conv", MC, CONV_A)
                dve.wait_ge(*taken["ah", n.up("ah")])
                for i in range(2):
                    j = 2 * b + i
                    bank = mine.full_bank(dve)
                    emptied(v.tensor_tensor(apT[:, j, 1:TOK + 1], bank[:, 0:TOK], ahT[:, j, :], ALU.mult))
                    link(v.tensor_scalar(acT[:, j, :], apT[:, j, 0:TOK], w[:, j, 0:1], None, ALU.mult))
                    for k in (1, 2):
                        link(v.scalar_tensor_tensor(out=acT[:, j, :], in0=apT[:, j, k:k + TOK], scalar=w[:, j, k:k + 1],
                                                    in1=acT[:, j, :], op0=ALU.mult, op1=ALU.add))

            def spatial(stage, t):
                if t == 0:
                    dve.wait_ge(*taken["u", n.up("u", 2)])
                b = C("b_spatial", MC, P)
                for j in range(MC):
                    bank = mine.full_bank(dve)
                    link(v.tensor_tensor(sp_t[0:64, :], bank[0:64, 0:P], b[0:64, j, :], ALU.add))
                    emptied(v.tensor_tensor(sp_t[64:128, :], bank[64:128, P:2 * P], b[64:128, j, :], ALU.add))
                    link(v.tensor_tensor(yT[:, MC + j, t * P:(t + 1) * P], sp_t[:, :], uT[:, j, t * P:(t + 1) * P], ALU.mult))

            def ab_cols(stage, b):
                for i in range(2):
                    j = 2 * b + i
                    bank = mine.full_bank(dve)
                    emptied(v.tensor_tensor(yT[:, j, :], bank[:, 0:TOK], acT[:, j, :], ALU.mult))

            def lam(stage):
                r = C("lam", 4, HD)
                link(*[v.tensor_tensor_reduce(out=sp_t[:, i * HD:(i + 1) * HD], in0=r[:, 2 * i, :], in1=r[:, 2 * i + 1, :],
                                              scale=1.0, scalar=0.0, op0=ALU.mult, op1=ALU.add,
                                              accum_out=stat[:, 12 + i:13 + i]) for i in range(1)])
                v.tensor_tensor_reduce(out=sp_t[:, HD:2 * HD], in0=r[:, 2, :], in1=r[:, 3, :], scale=1.0, scalar=0.0,
                                       op0=ALU.mult, op1=ALU.add, accum_out=stat[:, 13:14]).then_inc(lam_sums, 1)
                dve.wait_ge(lam_exps, 1)
                link(v.tensor_tensor(stat[:, 24:25], stat[:, 15:16], stat[:, 14:15], ALU.subtract))
                link(v.tensor_scalar(stat[:, 25:26], stat[:, 24:25], -LAM_INIT, None, ALU.add))

            def ca_cols(stage, b):
                if b == 0:
                    link(v.memset(cpT[:, :, 0:PAD_C], 0.0), v.memset(cpT[:, :, PAD_C + TOK:2 * PAD_C + TOK], 0.0))
                dve.wait_ge(*taken["cg", b + 1])
                for i in range(2):
                    j = 2 * b + i
                    bank = mine.full_bank(dve)
                    emptied(v.tensor_tensor(cpT[:, j, PAD_C:PAD_C + TOK], bank[:, 0:TOK], sgT[:, j, :], ALU.mult))

            def conv(stage):
                w, b = C("c_conv", MC, CONV_C), C("c_conv_b")
                link(*[v.tensor_scalar(ccT[:, j, :], cpT[:, j, 0:TOK], w[:, j, 0:1], b[:, j:j + 1], ALU.mult, ALU.add)
                       for j in range(MC)])
                for k in range(1, CONV_C):
                    ops = [v.scalar_tensor_tensor(out=ccT[:, j, :], in0=cpT[:, j, k:k + TOK], scalar=w[:, j, k:k + 1],
                                                  in1=ccT[:, j, :], op0=ALU.mult, op1=ALU.add) for j in range(MC)]
                    if k < CONV_C - 1:
                        link(*ops)
                    else:
                        link(*ops[:-1])
                        ops[-1].then_inc(cc_ready, 1)

            def norm_heads(tiles, scratch, gains):
                count = tiles.shape[1] * 8
                flat = tiles.rearrange("p a b -> p (a b)")
                heads = flat.rearrange("p (g d) -> p g d", d=HD)
                sqf = scratch.rearrange("p a b -> p (a b)")
                link(v.tensor_tensor(sqf, flat, flat, ALU.mult))
                link(v.tensor_reduce(ss_heads[:, 0:count], sqf.rearrange("p (g d) -> p g d", d=HD), AX_X, ALU.add))
                mean_root(root_heads[:, 0:count], ms_heads[:, 0:count], ss_heads[:, 0:count], HD)
                link(v.tensor_tensor(heads, heads, root_heads[:, 0:count].unsqueeze(2).to_broadcast([P, count, HD]), ALU.mult))
                g, at, ops = C("qk_g", 2, HD), 0, []
                for groups, row in gains:
                    some = heads[:, at:at + groups, :]
                    ops.append(v.tensor_tensor(some, some, g[:, row:row + 1, :].to_broadcast([P, groups, HD]), ALU.mult))
                    at += groups
                return ops

            def ctx_keys(stage):
                dve.wait_ge(*taken["ctx rows"])
                norm_heads(kvc[:, 0:2, :], sqc[:, :, :], [(16, 1)])[0].then_inc(kc_normed, 1)

            def qk_norm(stage):
                dve.wait_ge(*taken["rows"])
                link(*norm_heads(qk[:, :, :], sq[:, :, :], [(16, 0), (16, 1)]))
                for i in range(2):
                    for t in range(TT):
                        two = qk[:, 2 * i + t, :].rearrange("p (g d two) -> p g d two", two=2, d=32)
                        even, odd = two[:, :, :, 0], two[:, :, :, 1]
                        cs = C("cos", TT, 32)[:, t:t + 1, :].to_broadcast([P, 8, 32])
                        sn = C("sin", TT, 32)[:, t:t + 1, :].to_broadcast([P, 8, 32])
                        tmp = [sq[:, 2 * t + q // 2, (q % 2) * 256:(q % 2 + 1) * 256].rearrange("p (g d) -> p g d", g=8)
                               for q in range(4)]
                        link(v.tensor_tensor(tmp[0], even, cs, ALU.mult), v.tensor_tensor(tmp[1], odd, sn, ALU.mult),
                             v.tensor_tensor(tmp[2], even, sn, ALU.mult), v.tensor_tensor(tmp[3], odd, cs, ALU.mult))
                        a = v.tensor_tensor(even, tmp[0], tmp[1], ALU.subtract)
                        b = v.tensor_tensor(odd, tmp[2], tmp[3], ALU.add)
                        if i == 1 and t == TT - 1:
                            link(a)
                            b.then_inc(roped, 1)
                        else:
                            link(a, b)

            def attend(stage, i):
                if i < TT * HEADS:
                    p = i % 2
                    for m in range(2):
                        dve.wait_ge(dve_bank_full, mine.n + m + 1)
                        link(v.tensor_reduce(smax[:, p, m:m + 1], psum[:, 5 + (mine.n + m) % 3, :], AX_X, ALU.max))
                    v.tensor_scalar(nmax[:, p, :], smax[:, p, :], -HD ** -0.5, None, ALU.mult).then_inc(nmax_ready, 1)
                    dve.wait_ge(prob_ready, i + 1)
                    emptied(v.reciprocal(prec[:, p, :], psums[:, p, :]))
                    emptied(v.tensor_scalar(prec[:, p, 1:2], prec[:, p, 1:2], stat[:, 25:26], None, ALU.mult))
                    link(v.tensor_scalar(prob[:, p, 0, :], prob[:, p, 0, :], prec[:, p, 0:1], None, ALU.mult))
                    v.scalar_tensor_tensor(out=prob[:, p, 0, :], in0=prob[:, p, 1, :], scalar=prec[:, p, 1:2],
                                           in1=prob[:, p, 0, :], op0=ALU.mult, op1=ALU.add).then_inc(mixed_ready, 1)
                if i > 0:
                    t, h = (i - 1) // HEADS, (i - 1) % HEADS
                    bank = mine.full_bank(dve)
                    emptied(v.tensor_copy(orow[:, t, h * P:(h + 1) * P], bank[:, 0:P]))

            def conv_norm(stage):
                bank = mine.full_bank(dve)
                mine.emptied(v.tensor_scalar(rr_ms[:, :], bank[:, 0:TOK], 1.0 / MIX, EPS, ALU.mult, ALU.add))
                dve.wait_ge(dve_took, mine.n)
                v.tensor_scalar(rr_ms[:, :], rr_ms[:, :], 1.0, None, ALU.mult).then_inc(ms_ready, 1)
                dve.wait_ge(root_ready, n.up("root"))
                link(v.reciprocal(rr_root[:, :], rr_root[:, :]))
                v.tensor_tensor(ccT[:, :, :], ccT[:, :, :], rr_root[:, :].unsqueeze(1).to_broadcast([P, MC, TOK]),
                                ALU.mult).then_inc(cn_ready, 1)

            def o_norm(stage, t):
                heads = orow[:, t, :].rearrange("p (h d) -> p h d", h=HEADS)
                sqo = sq[:, t, :]
                link(v.tensor_tensor(sqo, orow[:, t, :], orow[:, t, :], ALU.mult))
                link(v.tensor_reduce(stat[:, 28:32], sqo.rearrange("p (h d) -> p h d", h=HEADS), AX_X, ALU.add))
                mean_root(stat[:, 20:24], stat[:, 16:20], stat[:, 28:32], 2 * HD)
                link(v.tensor_tensor(heads, heads, stat[:, 20:24].unsqueeze(2).to_broadcast([P, HEADS, P]), ALU.mult))
                v.scalar_tensor_tensor(out=heads, in0=heads, scalar=1.0 - LAM_INIT,
                                       in1=C("subln_g").unsqueeze(1).to_broadcast([P, HEADS, P]),
                                       op0=ALU.mult, op1=ALU.mult).then_inc(on_ready, 1)

            def out_rows(stage, b):
                if b == 0:
                    dve.wait_ge(*taken["gate", stage, 0])
                s = slice(b * BLK, (b + 1) * BLK)
                for t in range(TT):
                    bank = mine.full_bank(dve)
                    tile = (TT if stage else 0) + t
                    emptied(v.tensor_tensor(xn[:, t, 0:BLK], bank[:, 0:BLK], gate_mix[:, s], ALU.mult))
                    link(v.tensor_tensor(x[:, tile, s], x[:, tile, s], xn[:, t, 0:BLK], ALU.add))

            def search(stage, h):
                k = n.up("scores")
                dve.wait_ge(*taken["scores", k])
                s = sc[:, (k - 1) % 2, :, :]
                val = sv[:, :].rearrange("p (q k) -> p q k", q=2 * TT)
                lists, tiles = range(2 * TT), range(TT)
                link(*[v.max(val[:, q, 0:8], s[:, q, :]) for q in lists])
                link(*[v.match_replace(sc_rest[:, q, :], val[:, q, 0:8], s[:, q, :], LOWEST) for q in lists])
                link(*[v.max(val[:, q, 8:16], sc_rest[:, q, :]) for q in lists])
                ops = [v.max_index(si[:, q, 8:16], val[:, q, 8:16], sc_rest[:, q, :]) for q in lists]
                ops += [v.max_index(si[:, q, 0:8], val[:, q, 0:8], s[:, q, :]) for q in lists]
                ops += [v.tensor_tensor(cand[:, t, :, :], val[:, t, :].unsqueeze(2).to_broadcast([P, TOPK, TOPK]),
                                        val[:, TT + t, :].unsqueeze(1).to_broadcast([P, TOPK, TOPK]), ALU.add) for t in tiles]
                link(*ops)
                flat = [cand[:, t, :, :].rearrange("p a b -> p (a b)") for t in tiles]
                link(*[v.max(cv[:, t, 0:8], flat[t]) for t in tiles])
                link(*[v.match_replace(cand_rest[:, t, :], cv[:, t, 0:8], flat[t], LOWEST) for t in tiles])
                link(*[v.max(cv[:, t, 8:16], cand_rest[:, t, :]) for t in tiles])
                v.tensor_tensor(e16[:, :, :], cv[:, :, :], cv[:, :, 0:1].to_broadcast([P, TT, TOPK]), ALU.subtract)\
                    .then_inc(cv_ready, 1)
                link(*[v.max_index(ci[:, t, 0:8], cv[:, t, 0:8], flat[t]) for t in tiles],
                     *[v.max_index(ci[:, t, 8:16], cv[:, t, 8:16], cand_rest[:, t, :]) for t in tiles],
                     v.tensor_copy(side[:, :, :], si[:, :, :]))
                link(v.tensor_scalar(pick[:, 0:TT, :], ci[:, :, :], 4, None, ALU.logical_shift_right),
                     v.tensor_scalar(pick[:, TT:, :], ci[:, :, :], 15, None, ALU.bitwise_and))
                link(v.tensor_copy(pos_f[:, :, :], pick[:, :, :]))
                shape = [P, 2 * TT, TOPK, TOPK]
                link(v.tensor_tensor(hot[:, :, :, :], pos_f[:, :, :].unsqueeze(3).to_broadcast(shape),
                                     C("iota").unsqueeze(1).unsqueeze(1).to_broadcast(shape), ALU.is_equal))
                link(v.tensor_tensor(hot[:, :, :, :], hot[:, :, :, :], side[:, :, :].unsqueeze(2).to_broadcast(shape), ALU.mult))
                link(v.tensor_reduce(side_no[:, :, :], hot[:, :, :, :], AX_X, ALU.add))
                cols = slice(h * TOPK, (h + 1) * TOPK)
                v.scalar_tensor_tensor(out=idx[:, stage % 2, :, cols], in0=side_no[:, 0:TT, :], scalar=float(PK),
                                       in1=side_no[:, TT:, :], op0=ALU.mult, op1=ALU.add).then_inc(idx_ready, 1)
                dve.wait_ge(exp_ready, k)
                link(v.tensor_reduce(e_stat[:, 0, :], e16[:, :, :], AX_X, ALU.add))
                link(v.reciprocal(e_stat[:, 1, :], e_stat[:, 0, :]))
                v.tensor_tensor(gw[:, stage % 2, :, cols], e16[:, :, :], e_stat[:, 1, :].unsqueeze(2).to_broadcast([P, TT, TOPK]),
                                ALU.mult).then_inc(sc_used, 1)
                dve.wait_ge(sc_used, k)

            steps = {"ada": ada_blk, "mods": mods, "gate": gate, "norm": norm, "norm_ctx": norm_ctx, "v_norm": v_norm,
                     "ac_cols": ac_cols, "spatial": spatial, "ab_cols": ab_cols, "lam": lam, "ca_cols": ca_cols,
                     "conv": conv, "ctx_keys": ctx_keys, "qk_norm": qk_norm, "attend": attend, "conv_norm": conv_norm,
                     "o_norm": o_norm, "out_rows": out_rows, "search": search}

            def dots_and_weights(T, it):
                stage, t = T // TT, T % TT

                def dot(c):
                    s = c % RING
                    dve.wait_ge(uv_landed[s], it * 16 + 16 * (T * NBODY + 1))
                    v.tensor_tensor_reduce(out=uv[:, s, 0:D], in0=uv[:, s, 0:D], in1=h2[:, stage % 2, t, :], scale=1.0, scalar=0.0,
                                           op0=ALU.mult, op1=ALU.add, accum_out=dots[:, c:c + 1]).then_inc(dots_ready, 1)

                def weigh(c):
                    s = c % RING
                    if c % GRP == 0:
                        dve.wait_ge(gelu_ready, it * (BODY // GRP) + (T * (NSEL // GRP) + c // GRP + 1))
                    dve.wait_ge(uv_used, it * BODY + (T * NSEL + c + 1))
                    v.tensor_scalar(diag[:, s, :], C("ident"), gel[:, c:c + 1], gw[:, stage % 2, t, bass.ds(it * BODY + c, 1)],
                                    ALU.mult, ALU.mult).then_inc(diag_ready, 1)

                for c in range(0, BODY, GRP):
                    for i in range(GRP):
                        dot(c + i)
                    if c:
                        for i in range(GRP):
                            weigh(c - GRP + i)
                for i in range(GRP):
                    weigh(BODY - GRP + i)

            def bodies(T, first, count):
                if count == 1:
                    dots_and_weights(T, first)
                    return
                with dve.Fori(first, first + count) as it:
                    dots_and_weights(T, it)

            def open_tile(T):
                stage, t = T // TT, T % TT
                dve.wait_ge(*taken["h2", stage, t])

            def close_tile(T):
                stage, t = T // TT, T % TT
                dve.wait_ge(acc_ready, T + 1)
                dve.wait_ge(*taken["gate", stage, 1])
                tmp = h2[:, stage % 2, t, :]
                v.tensor_tensor(tmp, acc.rearrange("p a b -> p (a b)"), gate_peer[:, stage % 2, :], ALU.mult).then_inc(acc_free, 1)
                dve.wait_ge(acc_free, T + 1)
                row = x[:, (TT if stage else 0) + t, :]
                done = v.tensor_tensor(row, row, tmp, ALU.add)
                if stage == 2:
                    done.then_inc(x_rows_ready, 1)
                else:
                    link(done)

            v.memset(ones[:, :], 1.0).then_inc(constants_set, 1)
            v.memset(zeros[:, :], 0.0).then_inc(constants_set, 1)
            dve.wait_ge(loaded, 16 * N_LOADS)
            walk(steps, open_tile, bodies, close_tile)


def in_columns(w):
    k, n = w.shape
    return w.reshape(k // P, P, n // BLK, BLK).transpose(2, 1, 0, 3).reshape(n // BLK, P, k // P * BLK)


def columns(a):
    a = a.reshape(-1, a.shape[-1] // P, P)
    return a.transpose(2, 0, 1).reshape(P, -1)


def rows_(a):
    return np.broadcast_to(a.reshape(1, -1), (P, a.size))


def kernel(x, c, ctx, c_ctx, w_ada, b_ada, norm1_g, norm2_g, w_in, w_out, a_conv_w, b_vnorm_g, b_spatial_w, b_spatial_b,
           c_conv_w, c_conv_b, c_norm_g, d_qk_norm_g, d_lambda, d_subln_g, peer_wq, peer_subkeys, peer_u, peer_v):
    import concourse.bacc as bacc
    from concourse.bass_utils import run_bass_kernel_spmd

    f = lambda a: np.asarray(a)
    x, c, ctx, c_ctx, w_ada, w_in, w_out, peer_wq = map(f, (x, c, ctx, c_ctx, w_ada, w_in, w_out, peer_wq))
    ts = f(b_spatial_w)[0].transpose(2, 0, 1)
    tok = np.arange(TOK)
    inv = (10000.0 ** (-np.arange(16, dtype=np.float32) / 16)).astype(np.float32)
    ang = np.concatenate([(tok // GRID_W).astype(np.float32)[:, None] * inv, (tok % GRID_W).astype(np.float32)[:, None] * inv], -1)
    table = lambda a: a.astype(np.float32).reshape(TT, P, 32).transpose(1, 0, 2).reshape(P, -1)
    part = {
        "ident": np.eye(P, dtype=np.float32),
        "iota": rows_(np.arange(TOPK, dtype=np.float32)),
        "cos": table(np.cos(ang)), "sin": table(np.sin(ang)),
        "c": np.stack([c[0], c_ctx], -1).reshape(KC, P, 2).transpose(1, 0, 2).reshape(P, -1),
        "b_ada": columns(f(b_ada)),
        "norm_g": columns(np.stack([f(norm1_g), f(norm2_g)], 1)),
        "a_conv": f(a_conv_w)[0].reshape(CONV_A, MC, P).transpose(2, 1, 0).reshape(P, -1),
        "c_conv": f(c_conv_w)[0].reshape(CONV_C, MC, P).transpose(2, 1, 0).reshape(P, -1),
        "c_conv_b": columns(f(c_conv_b)), "c_norm_g": columns(f(c_norm_g)),
        "vnorm_g": rows_(f(b_vnorm_g)), "qk_g": rows_(f(d_qk_norm_g)), "subln_g": rows_(f(d_subln_g)),
        "lam": rows_(f(d_lambda)),
        "b_spatial": np.repeat(f(b_spatial_b)[0].reshape(MC, 2, P).transpose(1, 0, 2), P // 2, axis=0).reshape(P, -1),
    }
    const = np.concatenate([part[name] for name, _ in PARTS], 1)
    wq = []
    for layer in range(2):
        keys = f(peer_subkeys)[layer].transpose(0, 3, 1, 2).reshape(PH, P, 2 * PK)
        wq.append(np.concatenate([in_columns(peer_wq[layer]), keys], 2))
    arrays = {
        "const": np.ascontiguousarray(const),
        "wst": np.ascontiguousarray(ts.transpose(0, 1, 2).reshape(P, -1)),
        "xin": np.concatenate([ctx[0].reshape(TT, P, D), x[0].reshape(TT, P, D)], 0),
        "ada": np.stack([in_columns(w_ada[i]) for i in range(2)]),
        "in": np.stack([in_columns(w_in[i]) for i in range(2)]),
        "out_w": np.stack([in_columns(w_out[i]) for i in range(2)]),
        "wq": np.stack(wq),
        "uv0": np.concatenate([f(peer_u)[0], f(peer_v)[0]], 1),
        "uv1": np.concatenate([f(peer_u)[1], f(peer_v)[1]], 1),
    }
    nc = bacc.Bacc("TRN2", target_bir_lowering=False, num_devices=1)
    A = {name: nc.dram_tensor(name + "_dram", a.shape, F32, kind="ExternalInput").ap() for name, a in arrays.items()}
    out = nc.dram_tensor("out_dram", (TT, P, D), F32, kind="ExternalOutput").ap()
    A["result"] = out
    build(nc, A)
    r = run_bass_kernel_spmd(nc, [{name + "_dram": a for name, a in arrays.items()}], core_ids=[0])
    return r.results[0]["out_dram"].reshape(1, TOK, D)
```

```python
import math
from contextlib import ExitStack

import numpy as np

import concourse.bass as bass
from concourse import mybir

F32 = mybir.dt.float32
U32 = mybir.dt.uint32
ALU = mybir.AluOpType
ACT = mybir.ActivationFunctionType
AX_X = mybir.AxisListType.X

P = 128
D = 1024
KC = D // P
TOK = 256
TT = TOK // P
MIX = 512
MC = MIX // P
GRID_W = 64
HEADS = 4
HD = 64
CONV_A = 3
CONV_C = 31
PAD_C = CONV_C // 2
N_ADA = 6
PH = 8
PK = 128
TOPK = 16
NSEL = PH * TOPK
EPS = 1e-6
LAM_INIT = 0.8 - 0.6 * math.exp(-0.3)
LOWEST = -3.4e38

BLK = 256
BLK_W = KC * BLK
SUB_W = 2 * PK
SLOT_W = BLK_W + SUB_W
WRING = 3
ADA_PAIRS = N_ADA * D // BLK // 2
CONV_STEP = 4

RING = 8
BODY = RING
NBODY = NSEL // BODY
GRP = 2

PARTS = [("ident", P), ("iota", TOPK), ("cos", TT * 32), ("sin", TT * 32), ("c", KC * 2), ("b_ada", 2 * 48),
         ("norm_g", 2 * 2 * KC), ("a_conv", MC * CONV_A), ("c_conv", MC * CONV_C), ("c_conv_b", MC),
         ("c_norm_g", MC), ("vnorm_g", MIX), ("qk_g", 2 * HD), ("subln_g", P), ("lam", 4 * HD),
         ("b_spatial", MC * P)]
AT, W_CONST = {}, 0
for _name, _w in PARTS:
    AT[_name] = (W_CONST, W_CONST + _w)
    W_CONST += _w

WEIGHTS = {"v_rows": ("in", 8), "u_cols": ("in", 6), "ah_cols": ("in", 0), "ac_cols": ("in", 2), "ab_cols": ("in", 4),
           "cg_cols": ("in", 2), "ca_cols": ("in", 0), "q_rows": ("in", 4), "k_rows": ("in", 6), "x_rows": ("in", 8),
           "kc_rows": ("in", 6), "vc_rows": ("in", 8), "out_rows": ("out", 0), "query": ("wq", 0)}


def pairs(stage, *names):
    return [(name, stage, b) for name in names for b in range(2)]


def both(*step):
    return [(*step, t) for t in range(TT)]


def deal(steps, more):
    out = []
    for i, step in enumerate(steps):
        out += [step] + more[len(more) * i // len(steps):len(more) * (i + 1) // len(steps)]
    return out


def ada(layer, first, last):
    return [("ada", layer, pair) for pair in range(first, last)]


def project_even(stage):
    return (pairs(stage, "v_rows") + [("v_norm", stage)] + pairs(stage, "u_cols", "ah_cols", "ac_cols") + both("spatial", stage)
            + pairs(stage, "ab_cols"))


def project_out(stage):
    return [("out_rows", stage, b) for b in range(D // BLK)]


def first_heads(stage):
    return [("query", stage, 0), ("query", stage, 1), ("search", stage, 0), ("query", stage, 2)]


def next_head(stage, h):
    return [("search", stage, h)] + ([("query", stage, h + 2)] if h < PH - 1 else [])


SHARE = {"ada": 9, "mods": 0, "gate": 3, "v_norm": 3, "spatial": 4, "norm": 8, "norm_ctx": 8, "turn_back": 2, "lam": 2,
         "conv": 9, "conv_norm": 6, "qk_norm": 8, "qk_turn": 2, "query": 10, "search": 14}


def schedule():
    before = {
        0: ada(0, 0, 4) + [("mods", 0, 0), ("norm", 0, 0)] + deal(project_even(0), ada(0, 4, 8)) + [("gate", 0, 0)]
        + deal(project_out(0), ada(0, 8, 10)) + [("mods", 0, 1), ("norm", 0, 1)] + both("turn_back", 0) + first_heads(0),
        1: [],
        2: [("norm_ctx", 2)] + pairs(2, "kc_rows", "vc_rows") + [("ctx_keys", 2)] + [("attend", 2, i) for i in range(TT * HEADS + 1)]
        + both("o_norm", 2) + project_out(2) + [("norm", 2, 1)] + both("turn_back", 2) + first_heads(2),
    }
    mixer_2 = ([("norm", 2, 0)] + pairs(2, "cg_cols", "ca_cols") + [("conv", 2, k) for k in range(0, CONV_C, CONV_STEP)]
               + [("conv_norm", 2)] + pairs(2, "q_rows") + [("qk_norm", 2, 0)] + pairs(2, "x_rows") + [("qk_turn", 2, 0)]
               + pairs(2, "k_rows") + [("qk_norm", 2, 1), ("qk_turn", 2, 1)])
    during = {
        0: ada(0, 10, 12) + [("gate", 0, 1), ("mods", 1, 0), ("gate", 1, 0), ("norm", 1, 0)] + project_even(1) + project_out(1)
        + [("mods", 1, 1), ("norm", 1, 1)] + both("turn_back", 1) + [("gate", 1, 1)] + ada(1, 0, 4) + first_heads(1),
        1: [("mods", 2, 0)] + deal(mixer_2, ada(1, 4, ADA_PAIRS)) + [("lam", 2), ("gate", 2, 0), ("mods", 2, 1), ("gate", 2, 1),
                                                                ("mods", 2, 2)],
        2: [],
    }
    program = []
    for stage in range(3):
        program += [("step", step) for step in before[stage]]
        own = [next_head(stage, h) for h in range(1, PH)]
        gaps = own + [[] for _ in range(TT * NBODY - len(own))]
        free = len(gaps) - 1 - len(own)
        total, spent = sum(SHARE.get(step[0], 7) for step in during[stage]), 0
        for step in during[stage]:
            gaps[len(own) + spent * free // (total + 1)].append(step)
            spent += SHARE.get(step[0], 7)
        for t in range(TT):
            T = stage * TT + t
            program.append(("open", T))
            h = 0
            while h < NBODY:
                k = 1
                while h + k < NBODY and not gaps[t * NBODY + h + k - 1]:
                    k += 1
                program.append(("bodies", T, h, k))
                h += k
                last = gaps[t * NBODY + h - 1]
                if h < NBODY:
                    program += [("step", step) for step in last]
            program.append(("close", T))
            program += [("step", step) for step in last]
    return program


def weight_blocks(program):
    order = []
    for item in program:
        if item[0] != "step":
            continue
        name, *args = item[1]
        if name == "ada":
            order += [("ada", args[0], 2 * args[1] + i) for i in range(2)]
        elif name in WEIGHTS and not (name == "query" and args[1] == PH):
            kind, first = WEIGHTS[name]
            order.append((kind, args[0] // 2, first + args[1]))
    return order


def build(nc, A):
    with ExitStack() as ctx:
        def sb(name, shape, dt=F32):
            return ctx.enter_context(nc.sbuf_tensor(name, shape, dt))

        def sem(name):
            return ctx.enter_context(nc.semaphore(name))

        const = sb("const", [P, W_CONST])
        wst = sb("wst", [P, 8 * P])
        ones = sb("ones", [P, P])
        zeros = sb("zeros", [P, 512], mybir.dt.bfloat16)
        x = sb("x", [P, 2 * TT, D])
        silu_c = sb("silu_c", [P, KC, 2])
        ada_c = sb("ada_c", [P, 2, 48, 2])
        ada_rows = sb("ada_rows", [2, 2, BLK])
        modg = sb("modg", [P, 3, KC])
        gate_mix = sb("gate_mix", [P, D])
        gate_peer = sb("gate_peer", [P, 2, D])
        gdiag = sb("gdiag", [P, 4, P])
        wring = sb("wring", [P, WRING, SLOT_W])
        hT = sb("hT", [P, KC, TOK])
        h2 = sb("h2", [P, 2, TT, D])
        stat = sb("stat", [P, 64])
        sp_t = sb("sp_t", [P, P])
        ss_heads, ms_heads, root_heads = (sb(s, [P, 16]) for s in ("ss_heads", "ms_heads", "root_heads"))
        smax, nmax, psums, prec = (sb(s, [P, 2, 2]) for s in ("smax", "nmax", "psums", "prec"))
        uv = sb("uv", [P, RING, 2 * D])
        diag = sb("diag", [P, RING, P])
        idx = sb("idx", [P, 2, TT, NSEL], U32)
        gw = sb("gw", [P, 2, TT, NSEL])
        stage_idx = sb("stage_idx", [P, 2, RING], U32)
        dots = sb("dots", [P, BODY])
        gel = sb("gel", [P, BODY])
        work = sb("work", [P, 8704])

        def view(base, off, *shape):
            n = int(np.prod(shape))
            flat = base[:, off:off + n]
            if len(shape) == 1:
                return flat
            if len(shape) == 2:
                return flat.rearrange("p (a b) -> p a b", a=shape[0])
            return flat.rearrange("p (a b c) -> p a b c", a=shape[0], b=shape[1])

        def C(name, *shape):
            a, b = AT[name]
            return view(const, a, *shape) if shape else const[:, a:b]

        xn = view(work, 0, 2, D)
        v_rows = view(work, 2048, TT, MIX)
        uT = view(work, 3072, MC, TOK)
        ahT = view(work, 4096, MC, TOK)
        apT = view(work, 5120, MC, TOK + 2)
        acT = view(work, 4096, MC, TOK)
        yT = view(work, 6656, 2 * MC, TOK)
        sgT = view(work, 2048, MC, TOK)
        cpT = view(work, 3072, MC, TOK + 2 * PAD_C)
        ccT = view(work, 4224, MC, TOK)
        csq = view(work, 2048, MC, TOK)
        rr_ms, rr_root = view(work, 5248, TOK), view(work, 5504, TOK)
        qT = view(work, 2048, HEADS, TOK)
        kxT = view(work, 3072, HEADS, TOK)
        vx = view(work, 4096, TT, MIX)
        qk = view(work, 5120, TT, MIX)
        sq = view(work, 7680, TT, MIX)
        ring = uv[:, :, :].rearrange("p a b -> p (a b)")
        hcT = view(ring, 0, KC, TOK)
        kvc = view(ring, 2048, 4, MIX)
        kcT = view(ring, 4096, HEADS, TOK)
        sqc = view(ring, 5120, 2, MIX)
        orow = view(ring, 6144, TT, MIX)
        prob = view(ring, 7168, 2, 2, MIX)
        pT = view(ring, 9216, 2, MIX)
        qh = view(work, 2048, 2, 2, TOK)
        sc = view(work, 3072, 2, 2 * TT, PK)
        sc_rest = view(work, 4096, 2 * TT, PK)
        cand = view(work, 4608, TT, TOPK, TOPK)
        cand_rest = view(work, 5120, TT, NSEL * 2)
        sv = view(work, 5632, 2 * TT * TOPK)
        cv = view(work, 5696, TT, TOPK)
        e16 = view(work, 5728, TT, TOPK)
        e_stat = view(work, 5760, 2, TT)
        side = view(work, 5764, 2 * TT, TOPK)
        pos_f = view(work, 5828, 2 * TT, TOPK)
        side_no = view(work, 5892, 2 * TT, TOPK)
        hot = view(work, 6656, 2 * TT, TOPK, TOPK)
        si = sb("si", [P, 2 * TT, TOPK], U32)
        ci = sb("ci", [P, TT, TOPK], U32)
        pick = sb("pick", [P, 2 * TT, TOPK], U32)

        psum = ctx.enter_context(nc.psum_tensor("psum", [P, 8, 512], F32))
        acc = psum[:, 0:2, :]

        loaded = sem("loaded")
        constants_set = sem("constants_set")
        w_landed = [sem(f"w_landed{i}") for i in range(WRING)]
        act_bank_full, act_took = sem("act_bank_full"), sem("act_took")
        dve_bank_full, dve_took = sem("dve_bank_full"), sem("dve_took")
        dve_chain = sem("dve_chain")
        silu_ready = sem("silu_ready")
        mods_ready = sem("mods_ready")
        gdiag_ready = sem("gdiag_ready")
        ms_ready, root_ready = sem("ms_ready"), sem("root_ready")
        xn_ready = sem("xn_ready")
        v_ready = sem("v_ready")
        sc_used = sem("sc_used")
        cv_ready, exp_ready = sem("cv_ready"), sem("exp_ready")
        idx_ready = sem("idx_ready")
        lam_sums, lam_exps = sem("lam_sums"), sem("lam_exps")
        kc_normed, roped = sem("kc_normed"), sem("roped")
        nmax_ready, prob_ready, mixed_ready = sem("nmax_ready"), sem("prob_ready"), sem("mixed_ready")
        cc_ready, csq_ready, cn_ready, conv_out = sem("cc_ready"), sem("csq_ready"), sem("cn_ready"), sem("conv_out")
        on_ready = sem("on_ready")
        staged, slot_claimed = sem("staged"), sem("slot_claimed")
        uv_landed = [sem(f"uv_landed{i}") for i in range(RING)]
        dots_ready, gelu_ready, diag_ready = sem("dots_ready"), sem("gelu_ready"), sem("diag_ready")
        uv_used = sem("uv_used")
        acc_ready, acc_free = sem("acc_ready"), sem("acc_free")
        x_rows_ready, out_stored = sem("x_rows_ready"), sem("out_stored")

        N_LOADS = 2 + 2 * TT
        program = schedule()
        blocks = weight_blocks(program)
        taken = {}
        multiplied = []
        block = ctx.enter_context(nc.Block())

        class Tally(dict):

            def up(self, what, by=1):
                self[what] = self.get(what, 0) + by
                return self[what]

        class Banks:

            def __init__(self, first, full, took):
                self.first, self.full, self.took, self.n = first, full, took, 0

            def bank(self):
                return psum[:, self.first + self.n % 3, :]

            def open(self, pe):
                if self.n >= 3:
                    pe.wait_ge(self.took, self.n - 2)
                return self.bank()

            def fill(self, last):
                last.then_inc(self.full, 1)
                self.n += 1

            def full_bank(self, reader):
                reader.wait_ge(self.full, self.n + 1)
                return self.bank()

            def emptied(self, last):
                last.then_inc(self.took, 1)
                self.n += 1

        def act_banks():
            return Banks(2, act_bank_full, act_took)

        def dve_banks():
            return Banks(5, dve_bank_full, dve_took)

        def shift(stage, which):
            j = 3 if which == 1 else 0
            return ada_c[:, stage // 2, j * KC:(j + 1) * KC, 1 if stage == 1 or which == 2 else 0]

        def tile_of(stage, t):
            return t if stage == 1 else TT + t

        def walk(steps, open_tile, bodies, close_tile):
            for kind, what, *more in program:
                if kind == "step":
                    if what[0] in steps:
                        steps[what[0]](*what[1:])
                elif kind == "open":
                    open_tile(what)
                elif kind == "close":
                    close_tile(what)
                else:
                    bodies(what, *more)

        @block.tensor
        def _(pe):
            n = Tally()
            to_act, to_dve = act_banks(), dve_banks()
            mm, turn = nc.tensor.matmul, nc.tensor.transpose
            ident = C("ident")

            def weights():
                k = n.up("block") - 1
                pe.wait_ge(w_landed[k % WRING], 16 * (k // WRING + 1))
                return wring[:, k % WRING, :]

            def kc(w):
                return w[:, 0:BLK_W].rearrange("p (k c) -> p k c", k=KC)

            def block_done(banks):
                multiplied.append((banks.full, banks.n))

            def ada_pair(layer, pair):
                if layer == 0 and pair == 0:
                    pe.wait_ge(silu_ready, 1)
                rows_at = []
                for i in range(2):
                    w = kc(weights())
                    bank = to_dve.open(pe)
                    for k in range(KC):
                        last = mm(bank[0:2, 0:BLK], silu_c[:, k, :], w[:, k, :], start=(k == 0), stop=(k == KC - 1))
                    to_dve.fill(last)
                    block_done(to_dve)
                    rows_at.append(to_dve.n)
                bank = to_dve.open(pe)
                for i in range(2):
                    pe.wait_ge(dve_took, rows_at[i])
                    for j in range(2):
                        o = 4 * i + 2 * j
                        last = mm(bank[:, o:o + 2], ada_rows[:, i, j * P:(j + 1) * P], ident[0:2, 0:2], start=True, stop=True)
                to_dve.fill(last)

            def gate(stage, which):
                for half in range(2):
                    pe.wait_ge(gdiag_ready, n.up("gdiag_ready"))
                    bank = to_act.open(pe)
                    for i in range(4):
                        last = mm(bank[:, i * P:(i + 1) * P], ones[:, :], gdiag[:, i, :], start=True, stop=True)
                    to_act.fill(last)
                    taken["gdiag", n["gdiag_ready"]] = (act_bank_full, to_act.n)
                taken["gate", stage, which] = (act_took, to_act.n)

            def turn_rows():
                k = n.up("xn_ready")
                pe.wait_ge(xn_ready, k)
                row = xn[:, (k - 1) % 2, :]
                for half, banks in ((0, to_act), (1, to_dve)):
                    bank = banks.open(pe)
                    for i in range(4):
                        c = half * 4 + i
                        last = turn(bank[:, i * P:(i + 1) * P], row[:, c * P:(c + 1) * P], ident)
                    banks.fill(last)
                n["hT"] = (to_act.n, to_dve.n)

            def norm(*_):
                for t in range(TT):
                    turn_rows()

            def wait_hT():
                pe.wait_ge(act_took, n["hT"][0])
                pe.wait_ge(dve_took, n["hT"][1])

            def token_major(banks, srcs):
                w = kc(weights())
                for src, t in srcs:
                    bank = banks.open(pe)
                    for k in range(KC):
                        last = mm(bank[:, 0:BLK], src[:, k, t * P:(t + 1) * P], w[:, k, :], start=(k == 0), stop=(k == KC - 1))
                    banks.fill(last)
                block_done(banks)

            def channel_major(banks):
                wait_hT()
                w = kc(weights())
                for i in range(2):
                    bank = banks.open(pe)
                    for k in range(KC):
                        last = mm(bank[:, 0:TOK], w[:, k, i * P:(i + 1) * P], hT[:, k, :], start=(k == 0), stop=(k == KC - 1))
                    banks.fill(last)
                block_done(banks)

            def v_project(stage, b):
                wait_hT()
                token_major(to_act, [(hT, t) for t in range(TT)])
                taken["v", n.up("v")] = (act_took, to_act.n)

            def noted(what):
                channel_major(to_act)
                taken[what, n.up(what)] = (act_took, to_act.n)

            def spatial(stage, t):
                pe.wait_ge(v_ready, n.up("v_ready"))
                for j in range(MC):
                    bank = to_dve.open(pe)
                    to_dve.fill(mm(bank[:, 0:2 * P], v_rows[:, t, j * P:(j + 1) * P], wst[:, j * 2 * P:(j + 1) * 2 * P],
                                   start=True, stop=True))

            def rows(src):
                wait_hT()
                token_major(to_act, [(src, t) for t in range(TT)])
                taken["rows", n.up("rows")] = (act_took, to_act.n)

            def turn_heads(tiles):
                for tile in tiles:
                    bank = to_act.open(pe)
                    for h in range(HEADS):
                        last = turn(bank[:, h * P:(h + 1) * P], tile[:, h * P:(h + 1) * P], ident)
                    to_act.fill(last)

            def ctx_keys(stage):
                taken["ctx rows"] = (act_took, to_act.n)
                pe.wait_ge(kc_normed, 1)
                turn_heads([kvc[:, i, :] for i in range(2)])
                n["kT"] = to_act.n

            def qk_turn(stage, i):
                pe.wait_ge(roped, i + 1)
                turn_heads([qk[:, t, :] for t in range(TT)])

            def attend(stage, i):
                if i == 0:
                    pe.wait_ge(act_took, n["kT"])
                if i < TT * HEADS:
                    t, h = i // HEADS, i % HEADS
                    taken["scores of", i] = (dve_bank_full, to_dve.n)
                    for m in range(2):
                        half = slice(m * HD, (m + 1) * HD)
                        bank = to_dve.open(pe)
                        for k, keys in enumerate((kxT, kcT)):
                            last = mm(bank[:, k * TOK:(k + 1) * TOK], qT[half, h, t * P:(t + 1) * P], keys[half, h, :],
                                      start=True, stop=True)
                        to_dve.fill(last)
                if i > 0:
                    h = (i - 1) % HEADS
                    pe.wait_ge(mixed_ready, i)
                    bank = to_act.open(pe)
                    for k in range(4):
                        last = turn(bank[:, k * P:(k + 1) * P], prob[:, (i - 1) % 2, 0, k * P:(k + 1) * P], ident)
                    to_act.fill(last)
                    pe.wait_ge(act_took, to_act.n)
                    bank = to_dve.open(pe)
                    for k, values in enumerate((vx[:, 0, :], vx[:, 1, :], kvc[:, 2, :], kvc[:, 3, :])):
                        last = mm(bank[:, 0:P], pT[:, (i - 1) % 2, k * P:(k + 1) * P], values[:, h * P:(h + 1) * P],
                                  start=(k == 0), stop=(k == 3))
                    to_dve.fill(last)

            def conv_norm(stage):
                pe.wait_ge(csq_ready, 1)
                bank = to_dve.open(pe)
                for j in range(MC):
                    last = mm(bank[:, 0:TOK], ones[:, :], csq[:, j, :], start=(j == 0), stop=(j == MC - 1))
                to_dve.fill(last)

            def o_norm(stage, t):
                pe.wait_ge(on_ready, t + 1)
                bank = to_act.open(pe)
                for h in range(HEADS):
                    last = turn(bank[:, h * P:(h + 1) * P], orow[:, t, h * P:(h + 1) * P], ident)
                to_act.fill(last)

            def out_rows(stage, b):
                if b == 0 and stage < 2:
                    pe.wait_ge(dve_took, to_dve.n)
                elif b == 0:
                    pe.wait_ge(act_took, to_act.n)
                    pe.wait_ge(conv_out, 1)
                token_major(to_dve, [(yT, t) for t in range(TT)])

            def turn_back(stage, t):
                wait_hT()
                for half in range(2):
                    bank = to_act.open(pe)
                    for i in range(4):
                        last = turn(bank[:, i * P:(i + 1) * P], hT[:, half * 4 + i, t * P:(t + 1) * P], ident)
                    to_act.fill(last)
                taken["h2", stage, t] = (act_took, to_act.n)

            def query(stage, h):
                if h > 0:
                    pe.wait_ge(act_took, n["qh"])
                    bank = to_act.open(pe)
                    for q in range(2):
                        for t in range(TT):
                            o = (q * TT + t) * P
                            last = mm(bank[:, o:o + P], qh[:, (h - 1) % 2, q, t * P:(t + 1) * P],
                                      n["wq"][:, BLK_W + q * PK:BLK_W + (q + 1) * PK], start=True, stop=True)
                    to_act.fill(last)
                    block_done(to_act)
                    taken["scores", n.up("scores")] = (act_took, to_act.n)
                if h < PH:
                    wait_hT()
                    n["wq"] = weights()
                    w = kc(n["wq"])
                    for q in range(2):
                        bank = to_act.open(pe)
                        for k in range(KC):
                            last = mm(bank[:, 0:TOK], w[:, k, q * P:(q + 1) * P], hT[:, k, :],
                                      start=(k == 0), stop=(k == KC - 1))
                        to_act.fill(last)
                    n["qh"] = to_act.n

            steps = {"ada": ada_pair, "gate": gate, "norm": norm, "norm_ctx": norm, "v_rows": v_project,
                     "u_cols": lambda stage, b: noted("u"), "ah_cols": lambda stage, b: noted("ah"),
                     "ac_cols": lambda stage, b: channel_major(to_dve), "ab_cols": lambda stage, b: channel_major(to_dve),
                     "spatial": spatial, "cg_cols": lambda stage, b: noted("cg"),
                     "ca_cols": lambda stage, b: channel_major(to_dve),
                     "q_rows": lambda stage, b: rows(hT), "k_rows": lambda stage, b: rows(hT), "x_rows": lambda stage, b: rows(hT),
                     "kc_rows": lambda stage, b: rows(hcT), "vc_rows": lambda stage, b: rows(hcT),
                     "ctx_keys": ctx_keys, "qk_turn": qk_turn, "attend": attend, "conv_norm": conv_norm, "o_norm": o_norm,
                     "out_rows": out_rows, "turn_back": turn_back, "query": query}

            def open_tile(T):
                if T:
                    pe.wait_ge(acc_free, T)
                for b in range(2):
                    mm(acc[:, b, :], zeros[:, 0:P], zeros[:, :], start=True, stop=False)

            def add_values(T, it):
                for c in range(BODY):
                    pe.wait_ge(diag_ready, it * BODY + (T * NSEL + c + 1))
                    for b in range(2):
                        last = mm(acc[:, b, :], diag[:, c % RING, :], uv[:, c % RING, D + 512 * b:D + 512 * (b + 1)],
                                  start=False, stop=False)
                    last.then_inc(uv_used, 1)

            def bodies(T, first, count):
                if count == 1:
                    add_values(T, first)
                    return
                with pe.Fori(first, first + count) as it:
                    add_values(T, it)

            def close_tile(T):
                for b in range(2):
                    last = mm(acc[:, b, :], zeros[:, 0:P], zeros[:, :], start=False, stop=True)
                last.then_inc(acc_ready, 1)

            pe.sem_inc(uv_used, RING)
            pe.wait_ge(constants_set, 2)
            pe.wait_ge(loaded, 16 * N_LOADS)
            walk(steps, open_tile, bodies, close_tile)

        @block.sync
        def _(sp):
            for dst, src in ((const[:, :], A["const"]), (wst[:, :], A["wst"])):
                sp.dma_start(dst, src).then_inc(loaded, 16)
            for i in range(2 * TT):
                sp.dma_start(x[:, i, :], A["xin"][i]).then_inc(loaded, 16)
            for n, (kind, layer, b) in enumerate(blocks):
                if n >= WRING:
                    sp.wait_ge(*multiplied[n - WRING])
                wide = SLOT_W if kind == "wq" else BLK_W
                sp.dma_start(wring[:, n % WRING, 0:wide], A[{"out": "out_w"}.get(kind, kind)][layer, b]).then_inc(w_landed[n % WRING], 16)
            for t in range(TT):
                sp.wait_ge(x_rows_ready, t + 1)
                sp.dma_start(A["result"][t], x[:, TT + t, :]).then_inc(out_stored, 16)
            sp.wait_ge(out_stored, 16 * TT)

        @block.gpsimd
        def _(pool):
            tables = [A["uv0"], A["uv1"]]

            def gathers(T, it):
                stage, t = T // TT, T % TT
                pool.wait_ge(idx_ready, it + (stage * PH + 1))
                pool.sem_inc(slot_claimed, 1)
                for half in range(2):
                    nc.gpsimd.tensor_copy(stage_idx[:, half, :],
                                          idx[:, stage % 2, t, bass.ds(it * TOPK + half * RING, RING)]).then_inc(staged, 1)
                    pool.wait_ge(staged, it * 2 + (T * PH * 2 + half + 1))
                    for s in range(RING):
                        pool.wait_ge(uv_used, it * TOPK + (T * NSEL + half * RING + s + 1))
                        pool.sem_inc(slot_claimed, 1)
                        nc.gpsimd.indirect_dma_start(
                            out=uv[:, s, :], out_offset=None, in_=tables[stage // 2],
                            in_offset=bass.IndirectOffsetOnAxis(ap=stage_idx[:, half, s:s + 1], axis=0),
                        ).then_inc(uv_landed[s], 16)

            for T in range(3 * TT):
                with pool.Fori(0, PH) as it:
                    gathers(T, it)

        @block.scalar
        def _(act):
            n = Tally()
            mine = act_banks()
            f = nc.scalar.activation

            def empty(dst, width, func=ACT.Copy, a=None, **kw):
                src = mine.full_bank(act)[:, 0:width]
                if a:
                    src = src.rearrange("p (a b) -> p a b", a=a)
                mine.emptied(f(dst, src, func, **kw))

            def root(dst, src):
                act.wait_ge(ms_ready, n.up("ms_ready"))
                f(dst, src, ACT.Sqrt).then_inc(root_ready, 1)

            def gate(stage, which):
                dst = gate_peer[:, stage % 2, :] if which else gate_mix
                for half in range(2):
                    empty(dst[:, half * 512:(half + 1) * 512], 512)

            def modulate(dst, t, stage, which):
                act.wait_ge(mods_ready, n["mods"])
                bank = mine.full_bank(act)
                for i in range(4):
                    last = f(dst[:, i, t * P:(t + 1) * P], bank[:, i * P:(i + 1) * P], ACT.Identity,
                             scale=modg[:, which, i:i + 1], bias=shift(stage, which)[:, i:i + 1])
                mine.emptied(last)

            def norm(stage, which):
                root(stat[:, 4:6], stat[:, 2:4])
                for t in range(TT):
                    modulate(hT, t, stage, which)

            def norm_ctx(stage):
                root(stat[:, 4:6], stat[:, 2:4])
                for t in range(TT):
                    modulate(hcT, t, 2, 2)

            def v_project(stage, b):
                for t in range(TT):
                    empty(v_rows[:, t, b * BLK:(b + 1) * BLK], BLK, ACT.Gelu_apprx_tanh)

            def v_norm(stage):
                root(stat[:, 10:12], stat[:, 8:10])

            def channels(dst, b, func):
                for i in range(2):
                    empty(dst[:, 2 * b + i, :], TOK, func)

            def rows(dst, b):
                for t in range(TT):
                    empty(dst[:, t, b * BLK:(b + 1) * BLK], BLK)

            def lam(stage):
                act.wait_ge(lam_sums, 1)
                f(stat[:, 14:16], stat[:, 12:14], ACT.Exp).then_inc(lam_exps, 1)

            def ctx_keys(stage):
                root(root_heads[:, :], ms_heads[:, :])
                for t in range(TT):
                    empty(kcT[:, :, t * P:(t + 1) * P], 4 * P, a=HEADS)

            def qk_norm(stage, i):
                root(root_heads[:, :], ms_heads[:, :])

            def qk_turn(stage, i):
                for t in range(TT):
                    empty((qT, kxT)[i][:, :, t * P:(t + 1) * P], 4 * P, a=HEADS)

            def attend(stage, i):
                if i < TT * HEADS:
                    act.wait_ge(nmax_ready, i + 1)
                    for m in range(2):
                        bank = psum[:, 5 + (taken["scores of", i][1] + m) % 3, :]
                        last = f(prob[:, i % 2, m, :], bank, ACT.Exp, scale=HD ** -0.5,
                                 bias=nmax[:, i % 2, m:m + 1], accum_out=psums[:, i % 2, m:m + 1])
                    last.then_inc(prob_ready, 1)
                if i > 0:
                    empty(pT[:, (i - 1) % 2, :], 4 * P)

            def conv_norm(stage):
                act.wait_ge(cc_ready, 1)
                f(csq[:, :, :], ccT[:, :, :], ACT.Square).then_inc(csq_ready, 1)
                root(rr_root[:, :], rr_ms[:, :])
                act.wait_ge(cn_ready, 1)
                for j in range(MC):
                    last = f(yT[:, j, :], ccT[:, j, :], ACT.Silu, scale=C("c_norm_g")[:, j:j + 1])
                last.then_inc(conv_out, 1)

            def o_norm(stage, t):
                root(stat[:, 20:24], stat[:, 16:20])
                empty(yT[:, MC:, t * P:(t + 1) * P], 4 * P, a=HEADS)

            def turn_back(stage, t):
                for half in range(2):
                    empty(h2[:, stage % 2, t, half * 512:(half + 1) * 512], 512)

            def query(stage, h):
                if h > 0:
                    k = n.up("scores")
                    if k > 2:
                        act.wait_ge(sc_used, k - 2)
                    empty(sc[:, (k - 1) % 2, :, :], 4 * P, a=4)
                if h < PH:
                    for q in range(2):
                        empty(qh[:, h % 2, q, :], TOK)

            def search(stage, h):
                act.wait_ge(cv_ready, n.up("cv"))
                f(e16[:, :, :], e16[:, :, :], ACT.Exp).then_inc(exp_ready, 1)

            def mods(stage, which):
                n.up("mods")

            steps = {"mods": mods, "gate": gate, "norm": norm, "norm_ctx": norm_ctx, "v_rows": v_project, "v_norm": v_norm,
                     "u_cols": lambda stage, b: channels(uT, b, ACT.Gelu_apprx_tanh),
                     "ah_cols": lambda stage, b: channels(ahT, b, ACT.Copy),
                     "cg_cols": lambda stage, b: channels(sgT, b, ACT.Sigmoid),
                     "q_rows": lambda stage, b: rows(qk, b), "k_rows": lambda stage, b: rows(qk, b),
                     "x_rows": lambda stage, b: rows(vx, b), "kc_rows": lambda stage, b: rows(kvc[:, 0:2, :], b),
                     "vc_rows": lambda stage, b: rows(kvc[:, 2:4, :], b), "ctx_keys": ctx_keys, "lam": lam,
                     "qk_norm": qk_norm, "qk_turn": qk_turn, "attend": attend, "conv_norm": conv_norm, "o_norm": o_norm,
                     "turn_back": turn_back, "query": query, "search": search}

            def gelus(T, it):
                for c in range(0, BODY, GRP):
                    act.wait_ge(dots_ready, it * BODY + (T * NSEL + c + GRP))
                    f(gel[:, c:c + GRP], dots[:, c:c + GRP], ACT.Gelu_apprx_tanh).then_inc(gelu_ready, 1)

            def bodies(T, first, count):
                if count == 1:
                    gelus(T, first)
                    return
                with act.Fori(first, first + count) as it:
                    gelus(T, it)

            act.wait_ge(loaded, 16 * N_LOADS)
            f(silu_c[:, :, :], C("c", KC, 2), ACT.Silu).then_inc(silu_ready, 1)
            walk(steps, lambda T: None, bodies, lambda T: None)

        @block.vector
        def _(dve):
            n = Tally()
            mine = dve_banks()
            v = nc.vector
            chain = [0]

            def link(*instructions):
                for ins in instructions:
                    ins.then_inc(dve_chain, 1)
                chain[0] += len(instructions)
                dve.wait_ge(dve_chain, chain[0])

            def emptied(ins):
                mine.emptied(ins)
                dve.wait_ge(dve_took, mine.n)

            def mean_root(dst, ms, ss, count):
                v.tensor_scalar(ms, ss, 1.0 / count, EPS, ALU.mult, ALU.add).then_inc(ms_ready, 1)
                dve.wait_ge(root_ready, n.up("root"))
                link(v.reciprocal(dst, dst))

            def ada_pair(layer, pair):
                for i in range(2):
                    bank = mine.full_bank(dve)
                    mine.emptied(v.tensor_copy(ada_rows[:, i, :], bank[0:2, 0:BLK]))
                bank = mine.full_bank(dve)[:, 0:8].rearrange("p (a b) -> p a b", a=4)
                bias = C("b_ada")[:, layer * 48 + 4 * pair:layer * 48 + 4 * pair + 4]
                emptied(v.tensor_tensor(ada_c[:, layer, 4 * pair:4 * pair + 4, :], bank, bias.unsqueeze(2).to_broadcast([P, 4, 2]),
                                        ALU.add))

            def mods(stage, which):
                j = 4 if which == 1 else 1
                own = 1 if stage == 1 or which == 2 else 0
                v.scalar_tensor_tensor(out=modg[:, which, :], in0=ada_c[:, stage // 2, j * KC:(j + 1) * KC, own], scalar=1.0,
                                       in1=C("norm_g", 4, KC)[:, 2 * (stage // 2) + which % 2, :],
                                       op0=ALU.add, op1=ALU.mult).then_inc(mods_ready, 1)
                dve.wait_ge(mods_ready, n.up("mods"))

            def gate(stage, which):
                own = 1 if stage == 1 else 0
                j = 5 if which else 2
                for half in range(2):
                    k = n.up("gdiag")
                    if k > 1:
                        dve.wait_ge(*taken["gdiag", k - 1])
                    for i in range(4):
                        c = j * KC + half * 4 + i
                        last = v.tensor_scalar(gdiag[:, i, :], C("ident"), ada_c[:, stage // 2, c, own:own + 1], None, ALU.mult)
                    last.then_inc(gdiag_ready, 1)

            def norm_rows(tiles, dst, stage, which):
                link(*[v.tensor_tensor_reduce(out=xn[:, t, :], in0=x[:, tile, :], in1=x[:, tile, :], scale=1.0, scalar=0.0,
                                              op0=ALU.mult, op1=ALU.add, accum_out=stat[:, t:t + 1]) for t, tile in enumerate(tiles)])
                mean_root(stat[:, 4:6], stat[:, 2:4], stat[:, 0:2], D)
                for t, tile in enumerate(tiles):
                    v.tensor_scalar(xn[:, t, :], x[:, tile, :], stat[:, 4 + t:5 + t], None, ALU.mult).then_inc(xn_ready, 1)
                for t in range(TT):
                    bank = mine.full_bank(dve)
                    for i in range(4):
                        last = v.tensor_scalar(dst[:, 4 + i, t * P:(t + 1) * P], bank[:, i * P:(i + 1) * P],
                                               modg[:, which, 4 + i:5 + i], shift(stage, which)[:, 4 + i:5 + i], ALU.mult, ALU.add)
                    emptied(last)

            def norm(stage, which):
                norm_rows([tile_of(stage, t) for t in range(TT)], hT, stage, which)

            def norm_ctx(stage):
                norm_rows(range(TT), hcT, 2, 2)

            def v_norm(stage):
                dve.wait_ge(*taken["v", n.up("v", 2)])
                link(*[v.tensor_tensor_reduce(out=yT[:, 2 * t:2 * t + 2, :].rearrange("p a b -> p (a b)"), in0=v_rows[:, t, :],
                                              in1=v_rows[:, t, :], scale=1.0, scalar=0.0, op0=ALU.mult, op1=ALU.add,
                                              accum_out=stat[:, 6 + t:7 + t]) for t in range(TT)])
                mean_root(stat[:, 10:12], stat[:, 8:10], stat[:, 6:8], MIX)
                for t in range(TT):
                    v.scalar_tensor_tensor(out=v_rows[:, t, :], in0=v_rows[:, t, :], scalar=stat[:, 10 + t:11 + t],
                                           in1=C("vnorm_g"), op0=ALU.mult, op1=ALU.mult).then_inc(v_ready, 1)
                link(v.memset(apT[:, :, 0:1], 0.0), v.memset(apT[:, :, TOK + 1:TOK + 2], 0.0))

            def ac_cols(stage, b):
                w = C("a_conv", MC, CONV_A)
                dve.wait_ge(*taken["ah", n.up("ah")])
                for i in range(2):
                    j = 2 * b + i
                    bank = mine.full_bank(dve)
                    emptied(v.tensor_tensor(apT[:, j, 1:TOK + 1], bank[:, 0:TOK], ahT[:, j, :], ALU.mult))
                    link(v.tensor_scalar(acT[:, j, :], apT[:, j, 0:TOK], w[:, j, 0:1], None, ALU.mult))
                    for k in (1, 2):
                        link(v.scalar_tensor_tensor(out=acT[:, j, :], in0=apT[:, j, k:k + TOK], scalar=w[:, j, k:k + 1],
                                                    in1=acT[:, j, :], op0=ALU.mult, op1=ALU.add))

            def spatial(stage, t):
                if t == 0:
                    dve.wait_ge(*taken["u", n.up("u", 2)])
                b = C("b_spatial", MC, P)
                for j in range(MC):
                    bank = mine.full_bank(dve)
                    link(v.tensor_tensor(sp_t[0:64, :], bank[0:64, 0:P], b[0:64, j, :], ALU.add))
                    emptied(v.tensor_tensor(sp_t[64:128, :], bank[64:128, P:2 * P], b[64:128, j, :], ALU.add))
                    link(v.tensor_tensor(yT[:, MC + j, t * P:(t + 1) * P], sp_t[:, :], uT[:, j, t * P:(t + 1) * P], ALU.mult))

            def ab_cols(stage, b):
                for i in range(2):
                    j = 2 * b + i
                    bank = mine.full_bank(dve)
                    emptied(v.tensor_tensor(yT[:, j, :], bank[:, 0:TOK], acT[:, j, :], ALU.mult))

            def lam(stage):
                r = C("lam", 4, HD)
                link(*[v.tensor_tensor_reduce(out=sp_t[:, i * HD:(i + 1) * HD], in0=r[:, 2 * i, :], in1=r[:, 2 * i + 1, :],
                                              scale=1.0, scalar=0.0, op0=ALU.mult, op1=ALU.add,
                                              accum_out=stat[:, 12 + i:13 + i]) for i in range(1)])
                v.tensor_tensor_reduce(out=sp_t[:, HD:2 * HD], in0=r[:, 2, :], in1=r[:, 3, :], scale=1.0, scalar=0.0,
                                       op0=ALU.mult, op1=ALU.add, accum_out=stat[:, 13:14]).then_inc(lam_sums, 1)
                dve.wait_ge(lam_exps, 1)
                link(v.tensor_tensor(stat[:, 24:25], stat[:, 15:16], stat[:, 14:15], ALU.subtract))
                link(v.tensor_scalar(stat[:, 25:26], stat[:, 24:25], -LAM_INIT, None, ALU.add))

            def ca_cols(stage, b):
                if b == 0:
                    link(v.memset(cpT[:, :, 0:PAD_C], 0.0), v.memset(cpT[:, :, PAD_C + TOK:2 * PAD_C + TOK], 0.0))
                dve.wait_ge(*taken["cg", b + 1])
                for i in range(2):
                    j = 2 * b + i
                    bank = mine.full_bank(dve)
                    emptied(v.tensor_tensor(cpT[:, j, PAD_C:PAD_C + TOK], bank[:, 0:TOK], sgT[:, j, :], ALU.mult))

            def conv(stage, first):
                w, b = C("c_conv", MC, CONV_C), C("c_conv_b")
                for k in range(first, min(first + CONV_STEP, CONV_C)):
                    if k == 0:
                        ops = [v.tensor_scalar(ccT[:, j, :], cpT[:, j, 0:TOK], w[:, j, 0:1], b[:, j:j + 1], ALU.mult, ALU.add)
                               for j in range(MC)]
                    else:
                        ops = [v.scalar_tensor_tensor(out=ccT[:, j, :], in0=cpT[:, j, k:k + TOK], scalar=w[:, j, k:k + 1],
                                                      in1=ccT[:, j, :], op0=ALU.mult, op1=ALU.add) for j in range(MC)]
                    if k < CONV_C - 1:
                        link(*ops)
                    else:
                        link(*ops[:-1])
                        ops[-1].then_inc(cc_ready, 1)

            def norm_heads(tiles, scratch, row):
                flat = tiles.rearrange("p a b -> p (a b)")
                heads = flat.rearrange("p (g d) -> p g d", d=HD)
                squares = scratch.rearrange("p a b -> p (a b)")
                link(v.tensor_tensor(squares, flat, flat, ALU.mult))
                link(v.tensor_reduce(ss_heads[:, :], squares.rearrange("p (g d) -> p g d", d=HD), AX_X, ALU.add))
                mean_root(root_heads[:, :], ms_heads[:, :], ss_heads[:, :], HD)
                link(v.tensor_tensor(heads, heads, root_heads[:, :].unsqueeze(2).to_broadcast([P, 16, HD]), ALU.mult))
                return v.tensor_tensor(heads, heads, C("qk_g", 2, HD)[:, row:row + 1, :].to_broadcast([P, 16, HD]), ALU.mult)

            def ctx_keys(stage):
                dve.wait_ge(*taken["ctx rows"])
                norm_heads(kvc[:, 0:2, :], sqc[:, :, :], 1).then_inc(kc_normed, 1)

            def qk_norm(stage, i):
                dve.wait_ge(*taken["rows", (2, 6)[i]])
                link(norm_heads(qk, sq, i))
                for t in range(TT):
                    two = qk[:, t, :].rearrange("p (g d two) -> p g d two", two=2, d=32)
                    even, odd = two[:, :, :, 0], two[:, :, :, 1]
                    cs = C("cos", TT, 32)[:, t:t + 1, :].to_broadcast([P, 8, 32])
                    sn = C("sin", TT, 32)[:, t:t + 1, :].to_broadcast([P, 8, 32])
                    tmp = [sq[:, q // 2, (q % 2) * 256:(q % 2 + 1) * 256].rearrange("p (g d) -> p g d", g=8) for q in range(4)]
                    link(v.tensor_tensor(tmp[0], even, cs, ALU.mult), v.tensor_tensor(tmp[1], odd, sn, ALU.mult),
                         v.tensor_tensor(tmp[2], even, sn, ALU.mult), v.tensor_tensor(tmp[3], odd, cs, ALU.mult))
                    link(v.tensor_tensor(even, tmp[0], tmp[1], ALU.subtract))
                    done = v.tensor_tensor(odd, tmp[2], tmp[3], ALU.add)
                    if t < TT - 1:
                        link(done)
                    else:
                        done.then_inc(roped, 1)

            def attend(stage, i):
                if i < TT * HEADS:
                    p = i % 2
                    for m in range(2):
                        dve.wait_ge(dve_bank_full, mine.n + m + 1)
                        link(v.tensor_reduce(smax[:, p, m:m + 1], psum[:, 5 + (mine.n + m) % 3, :], AX_X, ALU.max))
                    v.tensor_scalar(nmax[:, p, :], smax[:, p, :], -HD ** -0.5, None, ALU.mult).then_inc(nmax_ready, 1)
                    dve.wait_ge(prob_ready, i + 1)
                    emptied(v.reciprocal(prec[:, p, :], psums[:, p, :]))
                    emptied(v.tensor_scalar(prec[:, p, 1:2], prec[:, p, 1:2], stat[:, 25:26], None, ALU.mult))
                    link(v.tensor_scalar(prob[:, p, 0, :], prob[:, p, 0, :], prec[:, p, 0:1], None, ALU.mult))
                    v.scalar_tensor_tensor(out=prob[:, p, 0, :], in0=prob[:, p, 1, :], scalar=prec[:, p, 1:2],
                                           in1=prob[:, p, 0, :], op0=ALU.mult, op1=ALU.add).then_inc(mixed_ready, 1)
                if i > 0:
                    t, h = (i - 1) // HEADS, (i - 1) % HEADS
                    bank = mine.full_bank(dve)
                    emptied(v.tensor_copy(orow[:, t, h * P:(h + 1) * P], bank[:, 0:P]))

            def conv_norm(stage):
                bank = mine.full_bank(dve)
                mine.emptied(v.tensor_scalar(rr_ms[:, :], bank[:, 0:TOK], 1.0 / MIX, EPS, ALU.mult, ALU.add))
                dve.wait_ge(dve_took, mine.n)
                v.tensor_scalar(rr_ms[:, :], rr_ms[:, :], 1.0, None, ALU.mult).then_inc(ms_ready, 1)
                dve.wait_ge(root_ready, n.up("root"))
                link(v.reciprocal(rr_root[:, :], rr_root[:, :]))
                v.tensor_tensor(ccT[:, :, :], ccT[:, :, :], rr_root[:, :].unsqueeze(1).to_broadcast([P, MC, TOK]),
                                ALU.mult).then_inc(cn_ready, 1)

            def o_norm(stage, t):
                heads = orow[:, t, :].rearrange("p (h d) -> p h d", h=HEADS)
                sqo = sqc[:, t, :]
                link(v.tensor_tensor(sqo, orow[:, t, :], orow[:, t, :], ALU.mult))
                link(v.tensor_reduce(stat[:, 28:32], sqo.rearrange("p (h d) -> p h d", h=HEADS), AX_X, ALU.add))
                mean_root(stat[:, 20:24], stat[:, 16:20], stat[:, 28:32], 2 * HD)
                link(v.tensor_tensor(heads, heads, stat[:, 20:24].unsqueeze(2).to_broadcast([P, HEADS, P]), ALU.mult))
                v.scalar_tensor_tensor(out=heads, in0=heads, scalar=1.0 - LAM_INIT,
                                       in1=C("subln_g").unsqueeze(1).to_broadcast([P, HEADS, P]),
                                       op0=ALU.mult, op1=ALU.mult).then_inc(on_ready, 1)

            def out_rows(stage, b):
                if b == 0:
                    dve.wait_ge(*taken["gate", stage, 0])
                s = slice(b * BLK, (b + 1) * BLK)
                for t in range(TT):
                    bank = mine.full_bank(dve)
                    tile = tile_of(stage, t)
                    emptied(v.tensor_tensor(xn[:, t, 0:BLK], bank[:, 0:BLK], gate_mix[:, s], ALU.mult))
                    link(v.tensor_tensor(x[:, tile, s], x[:, tile, s], xn[:, t, 0:BLK], ALU.add))

            def search(stage, h):
                k = n.up("scores")
                dve.wait_ge(*taken["scores", k])
                s = sc[:, (k - 1) % 2, :, :]
                val = sv[:, :].rearrange("p (q k) -> p q k", q=2 * TT)
                lists, tiles = range(2 * TT), range(TT)
                link(*[v.max(val[:, q, 0:8], s[:, q, :]) for q in lists])
                link(*[v.match_replace(sc_rest[:, q, :], val[:, q, 0:8], s[:, q, :], LOWEST) for q in lists])
                link(*[v.max(val[:, q, 8:16], sc_rest[:, q, :]) for q in lists])
                ops = [v.max_index(si[:, q, 8:16], val[:, q, 8:16], sc_rest[:, q, :]) for q in lists]
                ops += [v.max_index(si[:, q, 0:8], val[:, q, 0:8], s[:, q, :]) for q in lists]
                ops += [v.tensor_tensor(cand[:, t, :, :], val[:, t, :].unsqueeze(2).to_broadcast([P, TOPK, TOPK]),
                                        val[:, TT + t, :].unsqueeze(1).to_broadcast([P, TOPK, TOPK]), ALU.add) for t in tiles]
                link(*ops)
                flat = [cand[:, t, :, :].rearrange("p a b -> p (a b)") for t in tiles]
                link(*[v.max(cv[:, t, 0:8], flat[t]) for t in tiles])
                link(*[v.match_replace(cand_rest[:, t, :], cv[:, t, 0:8], flat[t], LOWEST) for t in tiles])
                link(*[v.max(cv[:, t, 8:16], cand_rest[:, t, :]) for t in tiles])
                v.tensor_tensor(e16[:, :, :], cv[:, :, :], cv[:, :, 0:1].to_broadcast([P, TT, TOPK]), ALU.subtract)\
                    .then_inc(cv_ready, 1)
                link(*[v.max_index(ci[:, t, 0:8], cv[:, t, 0:8], flat[t]) for t in tiles],
                     *[v.max_index(ci[:, t, 8:16], cv[:, t, 8:16], cand_rest[:, t, :]) for t in tiles],
                     v.tensor_copy(side[:, :, :], si[:, :, :]))
                link(v.tensor_scalar(pick[:, 0:TT, :], ci[:, :, :], 4, None, ALU.logical_shift_right),
                     v.tensor_scalar(pick[:, TT:, :], ci[:, :, :], 15, None, ALU.bitwise_and))
                link(v.tensor_copy(pos_f[:, :, :], pick[:, :, :]))
                shape = [P, 2 * TT, TOPK, TOPK]
                link(v.tensor_tensor(hot[:, :, :, :], pos_f[:, :, :].unsqueeze(3).to_broadcast(shape),
                                     C("iota").unsqueeze(1).unsqueeze(1).to_broadcast(shape), ALU.is_equal))
                link(v.tensor_tensor(hot[:, :, :, :], hot[:, :, :, :], side[:, :, :].unsqueeze(2).to_broadcast(shape), ALU.mult))
                link(v.tensor_reduce(side_no[:, :, :], hot[:, :, :, :], AX_X, ALU.add))
                cols = slice(h * TOPK, (h + 1) * TOPK)
                v.scalar_tensor_tensor(out=idx[:, stage % 2, :, cols], in0=side_no[:, 0:TT, :], scalar=float(PK),
                                       in1=side_no[:, TT:, :], op0=ALU.mult, op1=ALU.add).then_inc(idx_ready, 1)
                dve.wait_ge(exp_ready, k)
                link(v.tensor_reduce(e_stat[:, 0, :], e16[:, :, :], AX_X, ALU.add))
                link(v.reciprocal(e_stat[:, 1, :], e_stat[:, 0, :]))
                v.tensor_tensor(gw[:, stage % 2, :, cols], e16[:, :, :], e_stat[:, 1, :].unsqueeze(2).to_broadcast([P, TT, TOPK]),
                                ALU.mult).then_inc(sc_used, 1)
                dve.wait_ge(sc_used, k)

            steps = {"ada": ada_pair, "mods": mods, "gate": gate, "norm": norm, "norm_ctx": norm_ctx, "v_norm": v_norm,
                     "ac_cols": ac_cols, "spatial": spatial, "ab_cols": ab_cols, "lam": lam, "ca_cols": ca_cols,
                     "conv": conv, "ctx_keys": ctx_keys, "qk_norm": qk_norm, "attend": attend, "conv_norm": conv_norm,
                     "o_norm": o_norm, "out_rows": out_rows, "search": search}

            def dots_and_weights(T, it):
                stage, t = T // TT, T % TT

                def dot(c):
                    s = c % RING
                    dve.wait_ge(uv_landed[s], it * 16 + 16 * (T * NBODY + 1))
                    v.tensor_tensor_reduce(out=uv[:, s, 0:D], in0=uv[:, s, 0:D], in1=h2[:, stage % 2, t, :], scale=1.0, scalar=0.0,
                                           op0=ALU.mult, op1=ALU.add, accum_out=dots[:, c:c + 1]).then_inc(dots_ready, 1)

                def weigh(c):
                    s = c % RING
                    if c % GRP == 0:
                        dve.wait_ge(gelu_ready, it * (BODY // GRP) + (T * (NSEL // GRP) + c // GRP + 1))
                    dve.wait_ge(uv_used, it * BODY + (T * NSEL + c + 1))
                    v.tensor_scalar(diag[:, s, :], C("ident"), gel[:, c:c + 1], gw[:, stage % 2, t, bass.ds(it * BODY + c, 1)],
                                    ALU.mult, ALU.mult).then_inc(diag_ready, 1)

                for c in range(0, BODY, GRP):
                    for i in range(GRP):
                        dot(c + i)
                    if c:
                        for i in range(GRP):
                            weigh(c - GRP + i)
                for i in range(GRP):
                    weigh(BODY - GRP + i)

            def bodies(T, first, count):
                if count == 1:
                    dots_and_weights(T, first)
                    return
                with dve.Fori(first, first + count) as it:
                    dots_and_weights(T, it)

            def open_tile(T):
                stage, t = T // TT, T % TT
                dve.wait_ge(*taken["h2", stage, t])

            def close_tile(T):
                stage, t = T // TT, T % TT
                dve.wait_ge(acc_ready, T + 1)
                dve.wait_ge(*taken["gate", stage, 1])
                tmp = h2[:, stage % 2, t, :]
                v.tensor_tensor(tmp, acc.rearrange("p a b -> p (a b)"), gate_peer[:, stage % 2, :], ALU.mult).then_inc(acc_free, 1)
                dve.wait_ge(acc_free, T + 1)
                row = x[:, tile_of(stage, t), :]
                done = v.tensor_tensor(row, row, tmp, ALU.add)
                if stage == 2:
                    done.then_inc(x_rows_ready, 1)
                else:
                    link(done)

            v.memset(ones[:, :], 1.0).then_inc(constants_set, 1)
            v.memset(zeros[:, :], 0.0).then_inc(constants_set, 1)
            dve.wait_ge(loaded, 16 * N_LOADS)
            walk(steps, open_tile, bodies, close_tile)


def in_columns(w):
    k, n = w.shape
    return w.reshape(k // P, P, n // BLK, BLK).transpose(2, 1, 0, 3).reshape(n // BLK, P, k // P * BLK)


def columns(a):
    a = a.reshape(-1, a.shape[-1] // P, P)
    return a.transpose(2, 0, 1).reshape(P, -1)


def rows_(a):
    return np.broadcast_to(a.reshape(1, -1), (P, a.size))


def kernel(x, c, ctx, c_ctx, w_ada, b_ada, norm1_g, norm2_g, w_in, w_out, a_conv_w, b_vnorm_g, b_spatial_w, b_spatial_b,
           c_conv_w, c_conv_b, c_norm_g, d_qk_norm_g, d_lambda, d_subln_g, peer_wq, peer_subkeys, peer_u, peer_v):
    import concourse.bacc as bacc
    from concourse.bass_utils import run_bass_kernel_spmd

    f = lambda a: np.asarray(a)
    x, c, ctx, c_ctx, w_ada, w_in, w_out, peer_wq = map(f, (x, c, ctx, c_ctx, w_ada, w_in, w_out, peer_wq))
    ts = f(b_spatial_w)[0].transpose(2, 0, 1)
    tok = np.arange(TOK)
    inv = (10000.0 ** (-np.arange(16, dtype=np.float32) / 16)).astype(np.float32)
    ang = np.concatenate([(tok // GRID_W).astype(np.float32)[:, None] * inv, (tok % GRID_W).astype(np.float32)[:, None] * inv], -1)
    table = lambda a: a.astype(np.float32).reshape(TT, P, 32).transpose(1, 0, 2).reshape(P, -1)
    part = {
        "ident": np.eye(P, dtype=np.float32),
        "iota": rows_(np.arange(TOPK, dtype=np.float32)),
        "cos": table(np.cos(ang)), "sin": table(np.sin(ang)),
        "c": np.stack([c[0], c_ctx], -1).reshape(KC, P, 2).transpose(1, 0, 2).reshape(P, -1),
        "b_ada": columns(f(b_ada)),
        "norm_g": columns(np.stack([f(norm1_g), f(norm2_g)], 1)),
        "a_conv": f(a_conv_w)[0].reshape(CONV_A, MC, P).transpose(2, 1, 0).reshape(P, -1),
        "c_conv": f(c_conv_w)[0].reshape(CONV_C, MC, P).transpose(2, 1, 0).reshape(P, -1),
        "c_conv_b": columns(f(c_conv_b)), "c_norm_g": columns(f(c_norm_g)),
        "vnorm_g": rows_(f(b_vnorm_g)), "qk_g": rows_(f(d_qk_norm_g)), "subln_g": rows_(f(d_subln_g)),
        "lam": rows_(f(d_lambda)),
        "b_spatial": np.repeat(f(b_spatial_b)[0].reshape(MC, 2, P).transpose(1, 0, 2), P // 2, axis=0).reshape(P, -1),
    }
    const = np.concatenate([part[name] for name, _ in PARTS], 1)
    wq = []
    for layer in range(2):
        keys = f(peer_subkeys)[layer].transpose(0, 3, 1, 2).reshape(PH, P, 2 * PK)
        wq.append(np.concatenate([in_columns(peer_wq[layer]), keys], 2))
    arrays = {
        "const": np.ascontiguousarray(const),
        "wst": np.ascontiguousarray(ts.transpose(0, 1, 2).reshape(P, -1)),
        "xin": np.concatenate([ctx[0].reshape(TT, P, D), x[0].reshape(TT, P, D)], 0),
        "ada": np.stack([in_columns(w_ada[i]) for i in range(2)]),
        "in": np.stack([in_columns(w_in[i]) for i in range(2)]),
        "out_w": np.stack([in_columns(w_out[i]) for i in range(2)]),
        "wq": np.stack(wq),
        "uv0": np.concatenate([f(peer_u)[0], f(peer_v)[0]], 1),
        "uv1": np.concatenate([f(peer_u)[1], f(peer_v)[1]], 1),
    }
    nc = bacc.Bacc("TRN2", target_bir_lowering=False, num_devices=1)
    A = {name: nc.dram_tensor(name + "_dram", a.shape, F32, kind="ExternalInput").ap() for name, a in arrays.items()}
    out = nc.dram_tensor("out_dram", (TT, P, D), F32, kind="ExternalOutput").ap()
    A["result"] = out
    build(nc, A)
    r = run_bass_kernel_spmd(nc, [{name + "_dram": a for name, a in arrays.items()}], core_ids=[0])
    return r.results[0]["out_dram"].reshape(1, TOK, D)
```

```python
import math
from contextlib import ExitStack

import numpy as np

import concourse.bass as bass
from concourse import mybir

F32 = mybir.dt.float32
U32 = mybir.dt.uint32
ALU = mybir.AluOpType
ACT = mybir.ActivationFunctionType
AX_X = mybir.AxisListType.X

P = 128
D = 1024
KC = D // P
TOK = 256
TT = TOK // P
MIX = 512
MC = MIX // P
GRID_W = 64
HEADS = 4
HD = 64
CONV_A = 3
CONV_C = 31
PAD_C = CONV_C // 2
N_ADA = 6
PH = 8
PK = 128
TOPK = 16
NSEL = PH * TOPK
EPS = 1e-6
LAM_INIT = 0.8 - 0.6 * math.exp(-0.3)
LOWEST = -3.4e38

BLK = 256
BLK_W = KC * BLK
SUB_W = 2 * PK
SLOT_W = BLK_W + SUB_W
WRING = 3
ADA_PAIRS = N_ADA * D // BLK // 2
CONV_STEP = 4

RING = 8
BODY = RING
NBODY = NSEL // BODY

PARTS = [("ident", P), ("iota", TOPK), ("cos", TT * 32), ("sin", TT * 32), ("c", KC * 2), ("b_ada", 2 * 48),
         ("norm_g", 2 * 2 * KC), ("a_conv", MC * CONV_A), ("c_conv", MC * CONV_C), ("c_conv_b", MC),
         ("c_norm_g", MC), ("vnorm_g", MIX), ("qk_g", 2 * HD), ("subln_g", P), ("lam", 4 * HD),
         ("b_spatial", MC * P)]
AT, W_CONST = {}, 0
for _name, _w in PARTS:
    AT[_name] = (W_CONST, W_CONST + _w)
    W_CONST += _w

WEIGHTS = {"v_rows": ("in", 8), "u_cols": ("in", 6), "ah_cols": ("in", 0), "ac_cols": ("in", 2), "ab_cols": ("in", 4),
           "cg_cols": ("in", 2), "ca_cols": ("in", 0), "q_rows": ("in", 4), "k_rows": ("in", 6), "x_rows": ("in", 8),
           "kc_rows": ("in", 6), "vc_rows": ("in", 8), "out_rows": ("out_w", 0), "query": ("wq", 0)}


def pairs(stage, *names):
    return [(name, stage, b) for name in names for b in range(2)]


def both(*step):
    return [(*step, t) for t in range(TT)]


def deal(steps, more):
    out = []
    for i, step in enumerate(steps):
        out += [step] + more[len(more) * i // len(steps):len(more) * (i + 1) // len(steps)]
    return out


def ada(layer, first, last):
    return [("ada", layer, pair) for pair in range(first, last)]


def project_even(stage):
    return (pairs(stage, "v_rows") + [("v_norm", stage)] + pairs(stage, "u_cols", "ah_cols", "ac_cols") + both("spatial", stage)
            + pairs(stage, "ab_cols"))


def project_out(stage):
    return [("out_rows", stage, b) for b in range(D // BLK)]


def first_heads(stage):
    return [("query", stage, 0), ("query", stage, 1), ("search", stage, 0)] + both("turn_back", stage) + [("query", stage, 2)]


def next_head(stage, h):
    return [("search", stage, h)] + ([("query", stage, h + 2)] if h < PH - 1 else [])


SHARE = {"ada": 9, "mods": 0, "gate": 3, "v_norm": 3, "spatial": 6, "rms": 5, "norm": 5, "out_half": 8, "turn_back": 2, "lam": 2,
         "conv": 9, "conv_norm": 6, "qk_norm": 8, "qk_turn": 2, "query": 10, "search": 14}


def schedule():
    before = {
        0: ada(0, 0, 2) + [("rms", 0)] + ada(0, 2, 4) + [("mods", 0, 0), ("norm", 0, 0)]
        + deal(project_even(0), ada(0, 4, 8)) + [("gate", 0, 0)]
        + project_out(0)[:2] + ada(0, 8, 9) + project_out(0)[2:] + [("rms", 0)] + ada(0, 9, 10) + [("mods", 0, 1), ("norm", 0, 1)]
        + first_heads(0),
        1: [],
        2: [("rms", 1), ("norm_ctx", 2)] + pairs(2, "kc_rows") + [("kc_norm", 2)] + pairs(2, "vc_rows") + [("kc_turn", 2)]
        + [("attend", 2, i) for i in range(HEADS + 2)] + [("o_norm", 2, 0)]
        + [("attend", 2, i) for i in range(HEADS + 2, TT * HEADS + 1)] + [("o_norm", 2, 1)] + both("o_turn", 2)
        + [("out_half", 2, 1, b) for b in range(2)] + [("rms", 2), ("norm", 2, 1)] + first_heads(2),
    }
    mixer_2 = ([("rms", 2), ("norm", 2, 0)] + pairs(2, "cg_cols", "ca_cols") + [("conv", 2, k) for k in range(0, CONV_C, CONV_STEP)]
               + [("conv_norm", 2)] + pairs(2, "q_rows") + [("qk_norm", 2, 0)] + pairs(2, "x_rows") + [("qk_turn", 2, 0)]
               + pairs(2, "k_rows") + [("qk_norm", 2, 1), ("qk_turn", 2, 1)])
    during = {
        0: ada(0, 10, 12) + [("gate", 0, 1), ("mods", 1, 0), ("gate", 1, 0), ("rms", 1), ("norm", 1, 0)]
        + project_even(1) + project_out(1) + [("mods", 1, 1), ("rms", 1), ("norm", 1, 1), ("gate", 1, 1)] + ada(1, 0, 4) + first_heads(1),
        1: [("mods", 2, 0)] + deal(mixer_2, ada(1, 4, ADA_PAIRS)) + [("gate", 2, 0), ("out_half", 2, 0, 0),
              ("lam", 2), ("mods", 2, 1), ("gate", 2, 1), ("out_half", 2, 0, 1), ("mods", 2, 2)],
        2: [],
    }
    program = []
    for stage in range(3):
        program += [("step", step) for step in before[stage]]
        own = [next_head(stage, h) for h in range(1, PH)]
        gaps = own + [[] for _ in range(TT * NBODY - len(own))]
        free = len(gaps) - 3 - len(own)
        share = [SHARE.get(step[0], 7) for step in during[stage]]
        for i, step in enumerate(during[stage]):
            gaps[len(own) + int((sum(share[:i]) + share[i] / 2) * free / sum(share))].append(step)
        for t in range(TT):
            T = stage * TT + t
            program.append(("open", T))
            h = 0
            while h < NBODY:
                k = 1
                while h + k < NBODY and not gaps[t * NBODY + h + k - 1]:
                    k += 1
                program.append(("bodies", T, h, k))
                h += k
                last = gaps[t * NBODY + h - 1]
                if h < NBODY:
                    program += [("step", step) for step in last]
            program.append(("close", T))
            program += [("step", step) for step in last]
    return program


def weight_blocks(program):
    order = []
    for item in program:
        if item[0] != "step":
            continue
        name, *args = item[1]
        if name == "ada":
            order += [("ada", args[0], 2 * args[1] + i) for i in range(2)]
        elif name == "out_half":
            order.append(("out2", 0, 2 * args[1] + args[2]))
        elif name in WEIGHTS and not (name == "query" and args[1] == PH):
            kind, first = WEIGHTS[name]
            order.append((kind, args[0] // 2, first + args[1]))
    return order


def build(nc, A):
    with ExitStack() as ctx:
        def sb(name, shape, dt=F32):
            return ctx.enter_context(nc.sbuf_tensor(name, shape, dt))

        def sem(name):
            return ctx.enter_context(nc.semaphore(name))

        const = sb("const", [P, W_CONST])
        wst = sb("wst", [P, 8 * P])
        ones = sb("ones", [P, P])
        zeros = sb("zeros", [P, 512], mybir.dt.bfloat16)
        x = sb("x", [P, 2 * TT, D])
        silu_c = sb("silu_c", [P, KC, 2])
        ada_c = sb("ada_c", [P, 2, 48, 2])
        ada_rows = sb("ada_rows", [2, 2, BLK])
        modg = sb("modg", [P, 3, KC])
        gate_mix = sb("gate_mix", [P, D])
        gate_peer = sb("gate_peer", [P, 2, D])
        gdiag = sb("gdiag", [P, 4, P])
        wring = sb("wring", [P, WRING, SLOT_W])
        hT = sb("hT", [P, KC, TOK])
        h2 = sb("h2", [P, 2, TT, D])
        ss_x, ms_x, rr_x, ss_v, ms_v, rr_v = (sb(s, [P, TT]) for s in ("ss_x", "ms_x", "rr_x", "ss_v", "ms_v", "rr_v"))
        ss_o, ms_o, rr_o = (sb(s, [P, HEADS]) for s in ("ss_o", "ms_o", "rr_o"))
        lam_dot, lam_exp, neg_lam = (sb(s, [P, 2]) for s in ("lam_dot", "lam_exp", "neg_lam"))
        sp_t = sb("sp_t", [P, P])
        ss_heads, ms_heads, root_heads = (sb(s, [P, 16]) for s in ("ss_heads", "ms_heads", "root_heads"))
        smax, nmax, psums, prec = (sb(s, [P, 2, 2]) for s in ("smax", "nmax", "psums", "prec"))
        uv = sb("uv", [P, RING, 2 * D])
        diag = sb("diag", [P, RING, P])
        idx = sb("idx", [P, 2, TT, NSEL], U32)
        gw = sb("gw", [P, 2, TT, NSEL])
        stage_idx = sb("stage_idx", [P, 2, RING], U32)
        dots = sb("dots", [P, BODY])
        gel = sb("gel", [P, BODY])
        work = sb("work", [P, 8704])

        def view(base, off, *shape):
            n = int(np.prod(shape))
            flat = base[:, off:off + n]
            if len(shape) == 1:
                return flat
            if len(shape) == 2:
                return flat.rearrange("p (a b) -> p a b", a=shape[0])
            return flat.rearrange("p (a b c) -> p a b c", a=shape[0], b=shape[1])

        def C(name, *shape):
            a, b = AT[name]
            return view(const, a, *shape) if shape else const[:, a:b]

        xn = view(work, 0, 2, D)
        v_rows = view(work, 2048, TT, MIX)
        uT = view(work, 3072, MC, TOK)
        ahT = view(work, 4096, MC, TOK)
        apT = view(work, 5120, MC, TOK + 2)
        acT = view(work, 4096, MC, TOK)
        yT = view(work, 6656, 2 * MC, TOK)
        sgT = view(work, 2048, MC, TOK)
        cpT = view(work, 3072, MC, TOK + 2 * PAD_C)
        ccT = view(work, 4224, MC, TOK)
        csq = view(work, 2048, MC, TOK)
        rr_ms, rr_root = view(work, 5248, TOK), view(work, 5504, TOK)
        qT = view(work, 2048, HEADS, TOK)
        kxT = view(work, 3072, HEADS, TOK)
        vx = view(work, 4096, TT, MIX)
        qk = view(work, 5120, TT, MIX)
        sq = view(work, 7680, TT, MIX)
        ring = uv[:, :, :].rearrange("p a b -> p (a b)")
        hcT = view(ring, 0, KC, TOK)
        kvc = view(ring, 2048, 4, MIX)
        kcT = view(ring, 4096, HEADS, TOK)
        sqc = view(ring, 5120, 2, MIX)
        orow = view(ring, 6144, TT, MIX)
        prob = view(ring, 7168, 2, 2, MIX)
        pT = view(ring, 9216, 2, MIX)
        qh = view(work, 2048, 2, 2, TOK)
        sc = view(work, 3072, 2, 2 * TT, PK)
        sc_rest = view(work, 4096, 2 * TT, PK)
        cand = view(work, 4608, TT, TOPK, TOPK)
        cand_rest = view(work, 5120, TT, NSEL * 2)
        sv = view(work, 5632, 2 * TT * TOPK)
        cv = view(work, 5696, TT, TOPK)
        e16 = view(work, 5728, TT, TOPK)
        e_stat = view(work, 5760, 2, TT)
        side = view(work, 5764, 2 * TT, TOPK)
        pos_f = view(work, 5828, 2 * TT, TOPK)
        side_no = view(work, 5892, 2 * TT, TOPK)
        hot = view(work, 6656, 2 * TT, TOPK, TOPK)
        si = sb("si", [P, 2 * TT, TOPK], U32)
        ci = sb("ci", [P, TT, TOPK], U32)
        pick = sb("pick", [P, 2 * TT, TOPK], U32)

        psum = ctx.enter_context(nc.psum_tensor("psum", [P, 8, 512], F32))
        acc = psum[:, 0:2, :]

        score_banks = [psum[:, 0:2, :], psum[:, 5:7, :]]
        value_bank = psum[:, 7, 0:P]

        const_loaded, x_loaded = sem("const_loaded"), sem("x_loaded")
        constants_set = sem("constants_set")
        w_landed = [sem(f"w_landed{i}") for i in range(WRING)]
        act_bank_full, act_took = sem("act_bank_full"), sem("act_took")
        dve_bank_full, dve_took = sem("dve_bank_full"), sem("dve_took")
        dve_chain = sem("dve_chain")
        silu_ready, mods_ready, gdiag_ready = sem("silu_ready"), sem("mods_ready"), sem("gdiag_ready")
        ms_ready, root_ready, xn_ready = sem("ms_ready"), sem("root_ready"), sem("xn_ready")
        v_ready = sem("v_ready")
        cc_ready, csq_ready, cn_ready, conv_out = sem("cc_ready"), sem("csq_ready"), sem("cn_ready"), sem("conv_out")
        lam_sums, lam_exps = sem("lam_sums"), sem("lam_exps")
        kc_normed, roped = sem("kc_normed"), sem("roped")
        scores_full, nmax_ready, prob_ready, mixed_ready = (
            sem(s) for s in ("scores_full", "nmax_ready", "prob_ready", "mixed_ready"))
        values_full, values_taken, on_ready = sem("values_full"), sem("values_taken"), sem("on_ready")
        cv_ready, exp_ready, idx_ready, sc_used = sem("cv_ready"), sem("exp_ready"), sem("idx_ready"), sem("sc_used")
        staged, slot_claimed = sem("staged"), sem("slot_claimed")
        uv_landed = [sem(f"uv_landed{i}") for i in range(RING)]
        dots_ready, gelu_ready, diag_ready, uv_used = sem("dots_ready"), sem("gelu_ready"), sem("diag_ready"), sem("uv_used")
        acc_ready, acc_free = sem("acc_ready"), sem("acc_free")
        x_rows_ready, out_stored = sem("x_rows_ready"), sem("out_stored")

        N_LOADS = 2 * TT + 1
        program = schedule()
        blocks = weight_blocks(program)
        taken = {}
        multiplied = []
        block = ctx.enter_context(nc.Block())

        class Tally(dict):

            def up(self, what, by=1):
                self[what] = self.get(what, 0) + by
                return self[what]

        class Banks:

            def __init__(self, first, full, took):
                self.first, self.full, self.took, self.n = first, full, took, 0

            def bank(self):
                return psum[:, self.first + self.n % 3, :]

            def open(self, pe):
                if self.n >= 3:
                    pe.wait_ge(self.took, self.n - 2)
                return self.bank()

            def fill(self, last):
                last.then_inc(self.full, 1)
                self.n += 1

            def full_bank(self, reader):
                reader.wait_ge(self.full, self.n + 1)
                return self.bank()

            def emptied(self, last):
                last.then_inc(self.took, 1)
                self.n += 1

        def act_banks():
            return Banks(2, act_bank_full, act_took)

        def dve_banks():
            return Banks(5, dve_bank_full, dve_took)

        def shift(stage, which):
            j = 3 if which == 1 else 0
            return ada_c[:, stage // 2, j * KC:(j + 1) * KC, 1 if stage == 1 or which == 2 else 0]

        def tile_of(stage, t):
            return t if stage == 1 else TT + t

        def walk(steps, open_tile, bodies, close_tile):
            for kind, what, *more in program:
                if kind == "step":
                    if what[0] in steps:
                        steps[what[0]](*what[1:])
                elif kind == "open":
                    open_tile(what)
                elif kind == "close":
                    close_tile(what)
                else:
                    bodies(what, *more)

        @block.tensor
        def _(pe):
            n = Tally()
            to_act, to_dve = act_banks(), dve_banks()
            mm, turn = nc.tensor.matmul, nc.tensor.transpose
            ident = C("ident")

            def weights():
                k = n.up("block") - 1
                pe.wait_ge(w_landed[k % WRING], 16 * (k // WRING + 1))
                return wring[:, k % WRING, :]

            def kc(w):
                return w[:, 0:BLK_W].rearrange("p (k c) -> p k c", k=KC)

            def block_done(banks):
                multiplied.append((banks.full, banks.n))

            def ada_pair(layer, pair):
                if layer == 0 and pair == 0:
                    pe.wait_ge(silu_ready, 1)
                rows_at = []
                for i in range(2):
                    w = kc(weights())
                    bank = to_dve.open(pe)
                    for k in range(KC):
                        last = mm(bank[0:2, 0:BLK], silu_c[:, k, :], w[:, k, :], start=(k == 0), stop=(k == KC - 1))
                    to_dve.fill(last)
                    block_done(to_dve)
                    rows_at.append(to_dve.n)
                bank = to_dve.open(pe)
                for i in range(2):
                    pe.wait_ge(dve_took, rows_at[i])
                    for j in range(2):
                        o = 4 * i + 2 * j
                        last = mm(bank[:, o:o + 2], ada_rows[:, i, j * P:(j + 1) * P], ident[0:2, 0:2], start=True, stop=True)
                to_dve.fill(last)

            def gate(stage, which):
                for half in range(2):
                    pe.wait_ge(gdiag_ready, n.up("gdiag_ready"))
                    bank = to_act.open(pe)
                    for i in range(4):
                        last = mm(bank[:, i * P:(i + 1) * P], ones[:, :], gdiag[:, i, :], start=True, stop=True)
                    to_act.fill(last)
                    taken["gdiag", n["gdiag_ready"]] = (act_bank_full, to_act.n)
                taken["gate", stage, which] = (act_took, to_act.n)

            def turn_rows():
                k = n.up("xn_ready")
                pe.wait_ge(xn_ready, k)
                row = xn[:, (k - 1) % 2, :]
                for half, banks in ((0, to_act), (1, to_dve)):
                    bank = banks.open(pe)
                    for i in range(4):
                        c = half * 4 + i
                        last = turn(bank[:, i * P:(i + 1) * P], row[:, c * P:(c + 1) * P], ident)
                    banks.fill(last)
                n["hT"] = (to_act.n, to_dve.n)

            def norm(*_):
                for t in range(TT):
                    turn_rows()

            def wait_hT():
                pe.wait_ge(act_took, n["hT"][0])
                pe.wait_ge(dve_took, n["hT"][1])

            def token_major(banks, srcs):
                w = kc(weights())
                for src, t in srcs:
                    bank = banks.open(pe)
                    for k in range(KC):
                        last = mm(bank[:, 0:BLK], src[:, k, t * P:(t + 1) * P], w[:, k, :], start=(k == 0), stop=(k == KC - 1))
                    banks.fill(last)
                block_done(banks)

            def channel_major(banks):
                wait_hT()
                w = kc(weights())
                for i in range(2):
                    bank = banks.open(pe)
                    for k in range(KC):
                        last = mm(bank[:, 0:TOK], w[:, k, i * P:(i + 1) * P], hT[:, k, :], start=(k == 0), stop=(k == KC - 1))
                    banks.fill(last)
                block_done(banks)

            def v_project(stage, b):
                wait_hT()
                token_major(to_act, [(hT, t) for t in range(TT)])
                taken["v", n.up("v")] = (act_took, to_act.n)

            def noted(what):
                channel_major(to_act)
                taken[what, n.up(what)] = (act_took, to_act.n)

            def spatial(stage, t):
                pe.wait_ge(x_loaded, 16 * N_LOADS)
                pe.wait_ge(v_ready, n.up("v_ready"))
                for j in range(MC):
                    bank = to_dve.open(pe)
                    to_dve.fill(mm(bank[:, 0:2 * P], v_rows[:, t, j * P:(j + 1) * P], wst[:, j * 2 * P:(j + 1) * 2 * P],
                                   start=True, stop=True))

            def rows(src):
                wait_hT()
                token_major(to_act, [(src, t) for t in range(TT)])
                taken["rows", n.up("rows")] = (act_took, to_act.n)

            def turn_heads(tiles):
                for tile in tiles:
                    bank = to_act.open(pe)
                    for h in range(HEADS):
                        last = turn(bank[:, h * P:(h + 1) * P], tile[:, h * P:(h + 1) * P], ident)
                    to_act.fill(last)

            def kc_norm(stage):
                taken["kc"] = (act_took, to_act.n)

            def kc_turn(stage):
                pe.wait_ge(kc_normed, 1)
                turn_heads([kvc[:, i, :] for i in range(2)])
                n["kT"] = to_act.n

            def qk_turn(stage, i):
                pe.wait_ge(roped, i + 1)
                turn_heads([qk[:, t, :] for t in range(TT)])

            def attend(stage, i):
                if i == 0:
                    pe.wait_ge(act_took, n["kT"])
                    pe.wait_ge(dve_took, to_dve.n)
                    pe.wait_ge(acc_free, stage * TT)
                for ahead in ([0, 1] if i == 0 else [i + 1] if i + 1 < TT * HEADS else []):
                    t, h = ahead // HEADS, ahead % HEADS
                    if ahead >= 2:
                        pe.wait_ge(prob_ready, ahead - 1)
                    for m in range(2):
                        half = slice(m * HD, (m + 1) * HD)
                        for k, keys in enumerate((kxT, kcT)):
                            last = mm(score_banks[ahead % 2][:, m, k * TOK:(k + 1) * TOK], qT[half, h, t * P:(t + 1) * P],
                                      keys[half, h, :], start=True, stop=True)
                    last.then_inc(scores_full, 1)
                if i > 0:
                    h = (i - 1) % HEADS
                    pe.wait_ge(mixed_ready, i)
                    bank = to_act.open(pe)
                    for k in range(4):
                        last = turn(bank[:, k * P:(k + 1) * P], prob[:, (i - 1) % 2, 0, k * P:(k + 1) * P], ident)
                    to_act.fill(last)
                    pe.wait_ge(act_took, to_act.n)
                    if i > 1:
                        pe.wait_ge(values_taken, i - 1)
                    for k, values in enumerate((vx[:, 0, :], vx[:, 1, :], kvc[:, 2, :], kvc[:, 3, :])):
                        last = mm(value_bank, pT[:, (i - 1) % 2, k * P:(k + 1) * P], values[:, h * P:(h + 1) * P],
                                  start=(k == 0), stop=(k == 3))
                    last.then_inc(values_full, 1)

            def conv_norm(stage):
                pe.wait_ge(csq_ready, 1)
                bank = to_dve.open(pe)
                for j in range(MC):
                    last = mm(bank[:, 0:TOK], ones[:, :], csq[:, j, :], start=(j == 0), stop=(j == MC - 1))
                to_dve.fill(last)

            def o_turn(stage, t):
                pe.wait_ge(on_ready, t + 1)
                bank = to_act.open(pe)
                for h in range(HEADS):
                    last = turn(bank[:, h * P:(h + 1) * P], orow[:, t, h * P:(h + 1) * P], ident)
                to_act.fill(last)

            def out_rows(stage, b):
                if b == 0:
                    pe.wait_ge(dve_took, to_dve.n)
                token_major(to_dve, [(yT, t) for t in range(TT)])

            def out_half(stage, half, b):
                if half == 0:
                    pe.wait_ge(conv_out, 1)
                else:
                    pe.wait_ge(act_took, to_act.n)
                w = weights()[:, 0:BLK_W].rearrange("p (k c) -> p k c", k=MC)
                for t in range(TT):
                    bank = to_dve.open(pe)
                    for k in range(MC):
                        last = mm(bank, yT[:, half * MC + k, t * P:(t + 1) * P], w[:, k, :], start=(k == 0), stop=(k == MC - 1))
                    to_dve.fill(last)
                block_done(to_dve)

            def turn_back(stage, t):
                wait_hT()
                for half in range(2):
                    bank = to_act.open(pe)
                    for i in range(4):
                        last = turn(bank[:, i * P:(i + 1) * P], hT[:, half * 4 + i, t * P:(t + 1) * P], ident)
                    to_act.fill(last)
                taken["h2", stage, t] = (act_took, to_act.n)

            def query(stage, h):
                if h > 0:
                    pe.wait_ge(act_took, n["qh"])
                    bank = to_act.open(pe)
                    for q in range(2):
                        for t in range(TT):
                            o = (q * TT + t) * P
                            last = mm(bank[:, o:o + P], qh[:, (h - 1) % 2, q, t * P:(t + 1) * P],
                                      n["wq"][:, BLK_W + q * PK:BLK_W + (q + 1) * PK], start=True, stop=True)
                    to_act.fill(last)
                    block_done(to_act)
                    taken["scores", n.up("scores")] = (act_took, to_act.n)
                if h < PH:
                    wait_hT()
                    n["wq"] = weights()
                    w = kc(n["wq"])
                    for q in range(2):
                        bank = to_act.open(pe)
                        for k in range(KC):
                            last = mm(bank[:, 0:TOK], w[:, k, q * P:(q + 1) * P], hT[:, k, :],
                                      start=(k == 0), stop=(k == KC - 1))
                        to_act.fill(last)
                    n["qh"] = to_act.n

            steps = {"ada": ada_pair, "gate": gate, "norm": norm, "norm_ctx": norm, "v_rows": v_project,
                     "u_cols": lambda stage, b: noted("u"), "ah_cols": lambda stage, b: noted("ah"),
                     "ac_cols": lambda stage, b: channel_major(to_dve), "ab_cols": lambda stage, b: channel_major(to_dve),
                     "spatial": spatial, "cg_cols": lambda stage, b: noted("cg"),
                     "ca_cols": lambda stage, b: channel_major(to_dve),
                     "q_rows": lambda stage, b: rows(hT), "k_rows": lambda stage, b: rows(hT), "x_rows": lambda stage, b: rows(hT),
                     "kc_rows": lambda stage, b: rows(hcT), "vc_rows": lambda stage, b: rows(hcT),
                     "kc_norm": kc_norm, "kc_turn": kc_turn, "qk_turn": qk_turn, "attend": attend, "conv_norm": conv_norm, "o_turn": o_turn,
                     "out_rows": out_rows, "out_half": out_half, "turn_back": turn_back, "query": query}

            def open_tile(T):
                if T:
                    pe.wait_ge(acc_free, T)
                for b in range(2):
                    mm(acc[:, b, :], zeros[:, 0:P], zeros[:, :], start=True, stop=False)

            def add_values(T, it):
                for c in range(BODY):
                    pe.wait_ge(diag_ready, it * BODY + (T * NSEL + c + 1))
                    for b in range(2):
                        last = mm(acc[:, b, :], diag[:, c % RING, :], uv[:, c % RING, D + 512 * b:D + 512 * (b + 1)],
                                  start=False, stop=False)
                    last.then_inc(uv_used, 1)

            def bodies(T, first, count):
                if count == 1:
                    add_values(T, first)
                    return
                with pe.Fori(first, first + count) as it:
                    add_values(T, it)

            def close_tile(T):
                for b in range(2):
                    last = mm(acc[:, b, :], zeros[:, 0:P], zeros[:, :], start=False, stop=True)
                last.then_inc(acc_ready, 1)

            pe.sem_inc(uv_used, RING)
            pe.wait_ge(constants_set, 2)
            pe.wait_ge(const_loaded, 16)
            walk(steps, open_tile, bodies, close_tile)

        @block.sync
        def _(sp):
            sp.dma_start(const[:, :], A["const"]).then_inc(const_loaded, 16)
            for n, (kind, layer, b) in enumerate(blocks):
                if n == WRING:
                    for i in (2, 3, 0, 1):
                        sp.dma_start(x[:, i, :], A["xin"][i]).then_inc(x_loaded, 16)
                    sp.dma_start(wst[:, :], A["wst"]).then_inc(x_loaded, 16)
                if n >= WRING:
                    sp.wait_ge(*multiplied[n - WRING])
                wide = SLOT_W if kind == "wq" else BLK_W
                sp.dma_start(wring[:, n % WRING, 0:wide], A[kind][layer, b]).then_inc(w_landed[n % WRING], 16)
            for t in range(TT):
                sp.wait_ge(x_rows_ready, t + 1)
                sp.dma_start(A["result"][t], x[:, TT + t, :]).then_inc(out_stored, 16)
            sp.wait_ge(out_stored, 16 * TT)

        @block.gpsimd
        def _(pool):
            tables = [A["uv0"], A["uv1"]]

            def gathers(T, it):
                stage, t = T // TT, T % TT
                pool.wait_ge(idx_ready, it * TT + (stage * PH * TT + t + 1))
                pool.sem_inc(slot_claimed, 1)
                for half in range(2):
                    nc.gpsimd.tensor_copy(stage_idx[:, half, :],
                                          idx[:, stage % 2, t, bass.ds(it * TOPK + half * RING, RING)]).then_inc(staged, 1)
                    pool.wait_ge(staged, it * 2 + (T * PH * 2 + half + 1))
                    for s in range(RING):
                        pool.wait_ge(uv_used, it * TOPK + (T * NSEL + half * RING + s + 1))
                        pool.sem_inc(slot_claimed, 1)
                        nc.gpsimd.indirect_dma_start(
                            out=uv[:, s, :], out_offset=None, in_=tables[stage // 2],
                            in_offset=bass.IndirectOffsetOnAxis(ap=stage_idx[:, half, s:s + 1], axis=0),
                        ).then_inc(uv_landed[s], 16)

            for T in range(3 * TT):
                with pool.Fori(0, PH) as it:
                    gathers(T, it)

        @block.scalar
        def _(act):
            n = Tally()
            mine = act_banks()
            f = nc.scalar.activation

            def empty(dst, width, func=ACT.Copy, a=None, **kw):
                src = mine.full_bank(act)[:, 0:width]
                if a:
                    src = src.rearrange("p (a b) -> p a b", a=a)
                mine.emptied(f(dst, src, func, **kw))

            def root(dst, src):
                act.wait_ge(ms_ready, n.up("ms_ready"))
                f(dst, src, ACT.Sqrt).then_inc(root_ready, 1)

            def gate(stage, which):
                dst = gate_peer[:, stage % 2, :] if which else gate_mix
                for half in range(2):
                    empty(dst[:, half * 512:(half + 1) * 512], 512)

            def modulate(dst, t, stage, which):
                act.wait_ge(mods_ready, n["mods"])
                bank = mine.full_bank(act)
                for i in range(4):
                    last = f(dst[:, i, t * P:(t + 1) * P], bank[:, i * P:(i + 1) * P], ACT.Identity,
                             scale=modg[:, which, i:i + 1], bias=shift(stage, which)[:, i:i + 1])
                mine.emptied(last)

            def rms(stage):
                root(rr_x[:, :], ms_x[:, :])

            def norm(stage, which):
                for t in range(TT):
                    modulate(hT, t, stage, which)

            def norm_ctx(stage):
                for t in range(TT):
                    modulate(hcT, t, 2, 2)

            def v_project(stage, b):
                for t in range(TT):
                    empty(v_rows[:, t, b * BLK:(b + 1) * BLK], BLK, ACT.Gelu_apprx_tanh)

            def v_norm(stage):
                root(rr_v[:, :], ms_v[:, :])

            def channels(dst, b, func):
                for i in range(2):
                    empty(dst[:, 2 * b + i, :], TOK, func)

            def rows(dst, b):
                for t in range(TT):
                    empty(dst[:, t, b * BLK:(b + 1) * BLK], BLK)

            def lam(stage):
                act.wait_ge(lam_sums, 2)
                f(lam_exp[:, :], lam_dot[:, :], ACT.Exp).then_inc(lam_exps, 1)

            def kc_norm(stage):
                root(root_heads[:, :], ms_heads[:, :])

            def kc_turn(stage):
                for t in range(TT):
                    empty(kcT[:, :, t * P:(t + 1) * P], 4 * P, a=HEADS)

            def qk_norm(stage, i):
                root(root_heads[:, :], ms_heads[:, :])

            def qk_turn(stage, i):
                for t in range(TT):
                    empty((qT, kxT)[i][:, :, t * P:(t + 1) * P], 4 * P, a=HEADS)

            def attend(stage, i):
                if i < TT * HEADS:
                    act.wait_ge(nmax_ready, i + 1)
                    for m in range(2):
                        last = f(prob[:, i % 2, m, :], score_banks[i % 2][:, m, :], ACT.Exp, scale=HD ** -0.5,
                                 bias=nmax[:, i % 2, m:m + 1], accum_out=psums[:, i % 2, m:m + 1])
                    last.then_inc(prob_ready, 1)
                if i > 0:
                    empty(pT[:, (i - 1) % 2, :], 4 * P)

            def conv_norm(stage):
                act.wait_ge(cc_ready, 1)
                f(csq[:, :, :], ccT[:, :, :], ACT.Square).then_inc(csq_ready, 1)
                root(rr_root[:, :], rr_ms[:, :])
                act.wait_ge(cn_ready, 1)
                for j in range(MC):
                    last = f(yT[:, j, :], ccT[:, j, :], ACT.Silu, scale=C("c_norm_g")[:, j:j + 1])
                last.then_inc(conv_out, 1)
                act.wait_ge(conv_out, 1)

            def o_norm(stage, t):
                root(rr_o[:, :], ms_o[:, :])

            def o_turn(stage, t):
                empty(yT[:, MC:, t * P:(t + 1) * P], 4 * P, a=HEADS)

            def turn_back(stage, t):
                for half in range(2):
                    empty(h2[:, stage % 2, t, half * 512:(half + 1) * 512], 512)

            def query(stage, h):
                if h > 0:
                    k = n.up("scores")
                    if k > 2:
                        act.wait_ge(sc_used, k - 2)
                    empty(sc[:, (k - 1) % 2, :, :], 4 * P, a=4)
                if h < PH:
                    for q in range(2):
                        empty(qh[:, h % 2, q, :], TOK)

            def search(stage, h):
                for e in ([e16[:, 0, :], e16[:, 1, :]] if h == 0 else [e16[:, :, :]]):
                    act.wait_ge(cv_ready, n.up("cv"))
                    f(e, e, ACT.Exp).then_inc(exp_ready, 1)

            def mods(stage, which):
                n.up("mods")

            steps = {"mods": mods, "gate": gate, "rms": rms, "norm": norm, "norm_ctx": norm_ctx, "v_rows": v_project, "v_norm": v_norm,
                     "u_cols": lambda stage, b: channels(uT, b, ACT.Gelu_apprx_tanh),
                     "ah_cols": lambda stage, b: channels(ahT, b, ACT.Copy),
                     "cg_cols": lambda stage, b: channels(sgT, b, ACT.Sigmoid),
                     "q_rows": lambda stage, b: rows(qk, b), "k_rows": lambda stage, b: rows(qk, b),
                     "x_rows": lambda stage, b: rows(vx, b), "kc_rows": lambda stage, b: rows(kvc[:, 0:2, :], b),
                     "vc_rows": lambda stage, b: rows(kvc[:, 2:4, :], b), "kc_norm": kc_norm, "kc_turn": kc_turn, "lam": lam,
                     "qk_norm": qk_norm, "qk_turn": qk_turn, "attend": attend, "conv_norm": conv_norm, "o_norm": o_norm, "o_turn": o_turn,
                     "turn_back": turn_back, "query": query, "search": search}

            def gelus(T, it):
                for c in range(BODY):
                    act.wait_ge(dots_ready, it * BODY + (T * NSEL + c + 1))
                    f(gel[:, c:c + 1], dots[:, c:c + 1], ACT.Gelu_apprx_tanh).then_inc(gelu_ready, 1)

            def bodies(T, first, count):
                if count == 1:
                    gelus(T, first)
                    return
                with act.Fori(first, first + count) as it:
                    gelus(T, it)

            act.wait_ge(const_loaded, 16)
            f(silu_c[:, :, :], C("c", KC, 2), ACT.Silu).then_inc(silu_ready, 1)
            walk(steps, lambda T: None, bodies, lambda T: None)

        @block.vector
        def _(dve):
            n = Tally()
            mine = dve_banks()
            v = nc.vector
            chain = [0]

            def link(*instructions):
                for ins in instructions:
                    ins.then_inc(dve_chain, 1)
                chain[0] += len(instructions)
                dve.wait_ge(dve_chain, chain[0])

            def emptied(ins):
                mine.emptied(ins)
                dve.wait_ge(dve_took, mine.n)

            def mean_root(dst, ms, ss, count):
                v.tensor_scalar(ms, ss, 1.0 / count, EPS, ALU.mult, ALU.add).then_inc(ms_ready, 1)
                dve.wait_ge(root_ready, n.up("root"))
                link(v.reciprocal(dst, dst))

            def ada_pair(layer, pair):
                for i in range(2):
                    bank = mine.full_bank(dve)
                    mine.emptied(v.tensor_copy(ada_rows[:, i, :], bank[0:2, 0:BLK]))
                bank = mine.full_bank(dve)[:, 0:8].rearrange("p (a b) -> p a b", a=4)
                bias = C("b_ada")[:, layer * 48 + 4 * pair:layer * 48 + 4 * pair + 4]
                emptied(v.tensor_tensor(ada_c[:, layer, 4 * pair:4 * pair + 4, :], bank, bias.unsqueeze(2).to_broadcast([P, 4, 2]),
                                        ALU.add))

            def mods(stage, which):
                j = 4 if which == 1 else 1
                own = 1 if stage == 1 or which == 2 else 0
                v.scalar_tensor_tensor(out=modg[:, which, :], in0=ada_c[:, stage // 2, j * KC:(j + 1) * KC, own], scalar=1.0,
                                       in1=C("norm_g", 4, KC)[:, 2 * (stage // 2) + which % 2, :],
                                       op0=ALU.add, op1=ALU.mult).then_inc(mods_ready, 1)
                dve.wait_ge(mods_ready, n.up("mods"))

            def gate(stage, which):
                own = 1 if stage == 1 else 0
                j = 5 if which else 2
                for half in range(2):
                    k = n.up("gdiag")
                    if k > 1:
                        dve.wait_ge(*taken["gdiag", k - 1])
                    for i in range(4):
                        c = j * KC + half * 4 + i
                        last = v.tensor_scalar(gdiag[:, i, :], C("ident"), ada_c[:, stage // 2, c, own:own + 1], None, ALU.mult)
                    last.then_inc(gdiag_ready, 1)

            def rms(stage):
                if n.up("rms") == 1:
                    dve.wait_ge(x_loaded, 16 * N_LOADS)
                rows = [x[:, tile_of(stage, t), :] for t in range(TT)]
                link(*[v.tensor_tensor_reduce(out=xn[:, t, :], in0=row, in1=row, scale=1.0, scalar=0.0,
                                              op0=ALU.mult, op1=ALU.add, accum_out=ss_x[:, t:t + 1]) for t, row in enumerate(rows)])
                mean_root(rr_x[:, :], ms_x[:, :], ss_x[:, :], D)
                for t, row in enumerate(rows):
                    v.tensor_scalar(xn[:, t, :], row, rr_x[:, t:t + 1], None, ALU.mult).then_inc(xn_ready, 1)

            def modulate(dst, stage, which):
                for t in range(TT):
                    bank = mine.full_bank(dve)
                    for i in range(4):
                        last = v.tensor_scalar(dst[:, 4 + i, t * P:(t + 1) * P], bank[:, i * P:(i + 1) * P],
                                               modg[:, which, 4 + i:5 + i], shift(stage, which)[:, 4 + i:5 + i], ALU.mult, ALU.add)
                    emptied(last)

            def norm(stage, which):
                modulate(hT, stage, which)

            def norm_ctx(stage):
                modulate(hcT, 2, 2)

            def v_norm(stage):
                dve.wait_ge(*taken["v", n.up("v", 2)])
                link(*[v.tensor_tensor_reduce(out=yT[:, 2 * t:2 * t + 2, :].rearrange("p a b -> p (a b)"), in0=v_rows[:, t, :],
                                              in1=v_rows[:, t, :], scale=1.0, scalar=0.0, op0=ALU.mult, op1=ALU.add,
                                              accum_out=ss_v[:, t:t + 1]) for t in range(TT)])
                mean_root(rr_v[:, :], ms_v[:, :], ss_v[:, :], MIX)
                for t in range(TT):
                    v.scalar_tensor_tensor(out=v_rows[:, t, :], in0=v_rows[:, t, :], scalar=rr_v[:, t:t + 1],
                                           in1=C("vnorm_g"), op0=ALU.mult, op1=ALU.mult).then_inc(v_ready, 1)
                link(v.memset(apT[:, :, 0:1], 0.0), v.memset(apT[:, :, TOK + 1:TOK + 2], 0.0))

            def ac_cols(stage, b):
                w = C("a_conv", MC, CONV_A)
                dve.wait_ge(*taken["ah", n.up("ah")])
                for i in range(2):
                    j = 2 * b + i
                    bank = mine.full_bank(dve)
                    emptied(v.tensor_tensor(apT[:, j, 1:TOK + 1], bank[:, 0:TOK], ahT[:, j, :], ALU.mult))
                    link(v.tensor_scalar(acT[:, j, :], apT[:, j, 0:TOK], w[:, j, 0:1], None, ALU.mult))
                    for k in (1, 2):
                        link(v.scalar_tensor_tensor(out=acT[:, j, :], in0=apT[:, j, k:k + TOK], scalar=w[:, j, k:k + 1],
                                                    in1=acT[:, j, :], op0=ALU.mult, op1=ALU.add))

            def spatial(stage, t):
                if t == 0:
                    dve.wait_ge(*taken["u", n.up("u", 2)])
                b = C("b_spatial", MC, P)
                for j in range(MC):
                    bank = mine.full_bank(dve)
                    link(v.tensor_tensor(sp_t[0:64, :], bank[0:64, 0:P], b[0:64, j, :], ALU.add))
                    emptied(v.tensor_tensor(sp_t[64:128, :], bank[64:128, P:2 * P], b[64:128, j, :], ALU.add))
                    link(v.tensor_tensor(yT[:, MC + j, t * P:(t + 1) * P], sp_t[:, :], uT[:, j, t * P:(t + 1) * P], ALU.mult))

            def ab_cols(stage, b):
                for i in range(2):
                    j = 2 * b + i
                    bank = mine.full_bank(dve)
                    emptied(v.tensor_tensor(yT[:, j, :], bank[:, 0:TOK], acT[:, j, :], ALU.mult))

            def lam(stage):
                r = C("lam", 4, HD)
                sums = [v.tensor_tensor_reduce(out=sp_t[:, i * HD:(i + 1) * HD], in0=r[:, 2 * i, :], in1=r[:, 2 * i + 1, :],
                                                scale=1.0, scalar=0.0, op0=ALU.mult, op1=ALU.add,
                                                accum_out=lam_dot[:, i:i + 1]) for i in range(2)]
                for done in sums:
                    done.then_inc(lam_sums, 1)
                dve.wait_ge(lam_exps, 1)
                link(v.tensor_tensor(neg_lam[:, 0:1], lam_exp[:, 1:2], lam_exp[:, 0:1], ALU.subtract))
                link(v.tensor_scalar(neg_lam[:, 1:2], neg_lam[:, 0:1], -LAM_INIT, None, ALU.add))

            def ca_cols(stage, b):
                if b == 0:
                    link(v.memset(cpT[:, :, 0:PAD_C], 0.0), v.memset(cpT[:, :, PAD_C + TOK:2 * PAD_C + TOK], 0.0))
                dve.wait_ge(*taken["cg", b + 1])
                for i in range(2):
                    j = 2 * b + i
                    bank = mine.full_bank(dve)
                    emptied(v.tensor_tensor(cpT[:, j, PAD_C:PAD_C + TOK], bank[:, 0:TOK], sgT[:, j, :], ALU.mult))

            def conv(stage, first):
                w, b = C("c_conv", MC, CONV_C), C("c_conv_b")
                for k in range(first, min(first + CONV_STEP, CONV_C)):
                    if k == 0:
                        ops = [v.tensor_scalar(ccT[:, j, :], cpT[:, j, 0:TOK], w[:, j, 0:1], b[:, j:j + 1], ALU.mult, ALU.add)
                               for j in range(MC)]
                    else:
                        ops = [v.scalar_tensor_tensor(out=ccT[:, j, :], in0=cpT[:, j, k:k + TOK], scalar=w[:, j, k:k + 1],
                                                      in1=ccT[:, j, :], op0=ALU.mult, op1=ALU.add) for j in range(MC)]
                    if k < CONV_C - 1:
                        link(*ops)
                    else:
                        link(*ops[:-1])
                        ops[-1].then_inc(cc_ready, 1)

            def norm_heads(tiles, scratch, row):
                flat = tiles.rearrange("p a b -> p (a b)")
                heads = flat.rearrange("p (g d) -> p g d", d=HD)
                squares = scratch.rearrange("p a b -> p (a b)")
                link(v.tensor_tensor(squares, flat, flat, ALU.mult))
                link(v.tensor_reduce(ss_heads[:, :], squares.rearrange("p (g d) -> p g d", d=HD), AX_X, ALU.add))
                mean_root(root_heads[:, :], ms_heads[:, :], ss_heads[:, :], HD)
                link(v.tensor_tensor(heads, heads, root_heads[:, :].unsqueeze(2).to_broadcast([P, 16, HD]), ALU.mult))
                return v.tensor_tensor(heads, heads, C("qk_g", 2, HD)[:, row:row + 1, :].to_broadcast([P, 16, HD]), ALU.mult)

            def kc_norm(stage):
                dve.wait_ge(*taken["kc"])
                norm_heads(kvc[:, 0:2, :], sqc[:, :, :], 1).then_inc(kc_normed, 1)

            def qk_norm(stage, i):
                dve.wait_ge(*taken["rows", (2, 6)[i]])
                link(norm_heads(qk, sq, i))
                for t in range(TT):
                    two = qk[:, t, :].rearrange("p (g d two) -> p g d two", two=2, d=32)
                    even, odd = two[:, :, :, 0], two[:, :, :, 1]
                    cs = C("cos", TT, 32)[:, t:t + 1, :].to_broadcast([P, 8, 32])
                    sn = C("sin", TT, 32)[:, t:t + 1, :].to_broadcast([P, 8, 32])
                    tmp = [sq[:, q // 2, (q % 2) * 256:(q % 2 + 1) * 256].rearrange("p (g d) -> p g d", g=8) for q in range(4)]
                    link(v.tensor_tensor(tmp[0], even, cs, ALU.mult), v.tensor_tensor(tmp[1], odd, sn, ALU.mult),
                         v.tensor_tensor(tmp[2], even, sn, ALU.mult), v.tensor_tensor(tmp[3], odd, cs, ALU.mult))
                    link(v.tensor_tensor(even, tmp[0], tmp[1], ALU.subtract))
                    done = v.tensor_tensor(odd, tmp[2], tmp[3], ALU.add)
                    if t < TT - 1:
                        link(done)
                    else:
                        done.then_inc(roped, 1)

            def take_values(i):
                t, h = i // HEADS, i % HEADS
                dve.wait_ge(values_full, i + 1)
                v.tensor_scalar(orow[:, t, h * P:(h + 1) * P], value_bank, prec[:, i % 2, 0:1], None, ALU.mult)\
                    .then_inc(values_taken, 1)
                dve.wait_ge(values_taken, i + 1)

            def attend(stage, i):
                if i < TT * HEADS:
                    p = i % 2
                    dve.wait_ge(scores_full, i + 1)
                    link(v.tensor_reduce(smax[:, p, :], score_banks[p], AX_X, ALU.max))
                    v.tensor_scalar(nmax[:, p, :], smax[:, p, :], -HD ** -0.5, None, ALU.mult).then_inc(nmax_ready, 1)
                if i > 1:
                    take_values(i - 2)
                if i > 0:
                    p = (i - 1) % 2
                    dve.wait_ge(prob_ready, i)
                    link(v.reciprocal(prec[:, p, :], psums[:, p, :]))
                    link(v.tensor_scalar(prec[:, p, 1:2], prec[:, p, 1:2], psums[:, p, 0:1], neg_lam[:, 1:2], ALU.mult, ALU.mult))
                    v.scalar_tensor_tensor(out=prob[:, p, 0, :], in0=prob[:, p, 1, :], scalar=prec[:, p, 1:2],
                                           in1=prob[:, p, 0, :], op0=ALU.mult, op1=ALU.add).then_inc(mixed_ready, 1)
                if i == TT * HEADS:
                    take_values(i - 1)

            def conv_norm(stage):
                bank = mine.full_bank(dve)
                mine.emptied(v.tensor_scalar(rr_ms[:, :], bank[:, 0:TOK], 1.0 / MIX, EPS, ALU.mult, ALU.add))
                dve.wait_ge(dve_took, mine.n)
                v.tensor_scalar(rr_ms[:, :], rr_ms[:, :], 1.0, None, ALU.mult).then_inc(ms_ready, 1)
                dve.wait_ge(root_ready, n.up("root"))
                link(v.reciprocal(rr_root[:, :], rr_root[:, :]))
                v.tensor_tensor(ccT[:, :, :], ccT[:, :, :], rr_root[:, :].unsqueeze(1).to_broadcast([P, MC, TOK]),
                                ALU.mult).then_inc(cn_ready, 1)

            def o_norm(stage, t):
                heads = orow[:, t, :].rearrange("p (h d) -> p h d", h=HEADS)
                sqo = sqc[:, t, :]
                link(v.tensor_tensor(sqo, orow[:, t, :], orow[:, t, :], ALU.mult))
                link(v.tensor_reduce(ss_o[:, :], sqo.rearrange("p (h d) -> p h d", h=HEADS), AX_X, ALU.add))
                mean_root(rr_o[:, :], ms_o[:, :], ss_o[:, :], 2 * HD)
                link(v.tensor_tensor(heads, heads, rr_o[:, :].unsqueeze(2).to_broadcast([P, HEADS, P]), ALU.mult))
                v.scalar_tensor_tensor(out=heads, in0=heads, scalar=1.0 - LAM_INIT,
                                       in1=C("subln_g").unsqueeze(1).to_broadcast([P, HEADS, P]),
                                       op0=ALU.mult, op1=ALU.mult).then_inc(on_ready, 1)

            def add_gated(stage, s):
                for t in range(TT):
                    bank = mine.full_bank(dve)
                    tmp = xn[:, t, 0:s.stop - s.start]
                    row = x[:, tile_of(stage, t), s]
                    emptied(v.tensor_tensor(tmp, bank[:, 0:s.stop - s.start], gate_mix[:, s], ALU.mult))
                    link(v.tensor_tensor(row, row, tmp, ALU.add))

            def out_rows(stage, b):
                if b == 0:
                    dve.wait_ge(*taken["gate", stage, 0])
                add_gated(stage, slice(b * BLK, (b + 1) * BLK))

            def out_half(stage, half, b):
                if half == 0 and b == 0:
                    dve.wait_ge(*taken["gate", stage, 0])
                add_gated(stage, slice(b * 512, (b + 1) * 512))

            def find(stage, h, tiles):
                k = n["scores"]
                a, b = tiles[0], tiles[-1] + 1
                s = sc[:, (k - 1) % 2, :, :]
                val = sv[:, :].rearrange("p (q k) -> p q k", q=2 * TT)
                lists = [q * TT + t for q in range(2) for t in tiles]
                link(*[v.max(val[:, q, 0:8], s[:, q, :]) for q in lists])
                link(*[v.match_replace(sc_rest[:, q, :], val[:, q, 0:8], s[:, q, :], LOWEST) for q in lists])
                link(*[v.max(val[:, q, 8:16], sc_rest[:, q, :]) for q in lists])
                ops = [v.max_index(si[:, q, 8:16], val[:, q, 8:16], sc_rest[:, q, :]) for q in lists]
                ops += [v.max_index(si[:, q, 0:8], val[:, q, 0:8], s[:, q, :]) for q in lists]
                ops += [v.tensor_tensor(cand[:, t, :, :], val[:, t, :].unsqueeze(2).to_broadcast([P, TOPK, TOPK]),
                                        val[:, TT + t, :].unsqueeze(1).to_broadcast([P, TOPK, TOPK]), ALU.add) for t in tiles]
                link(*ops)
                flat = {t: cand[:, t, :, :].rearrange("p a b -> p (a b)") for t in tiles}
                link(*[v.max(cv[:, t, 0:8], flat[t]) for t in tiles])
                link(*[v.match_replace(cand_rest[:, t, :], cv[:, t, 0:8], flat[t], LOWEST) for t in tiles])
                link(*[v.max(cv[:, t, 8:16], cand_rest[:, t, :]) for t in tiles])
                v.tensor_tensor(e16[:, a:b, :], cv[:, a:b, :], cv[:, a:b, 0:1].to_broadcast([P, b - a, TOPK]), ALU.subtract)\
                    .then_inc(cv_ready, 1)
                link(*[v.max_index(ci[:, t, 0:8], cv[:, t, 0:8], flat[t]) for t in tiles],
                     *[v.max_index(ci[:, t, 8:16], cv[:, t, 8:16], cand_rest[:, t, :]) for t in tiles])

                def of(buffer):
                    return buffer[:, :, :].rearrange("p (q t) k -> p q t k", q=2)[:, :, a:b, :]

                link(v.tensor_copy(of(side), of(si)),
                     v.tensor_scalar(pick[:, a:b, :], ci[:, a:b, :], 4, None, ALU.logical_shift_right),
                     v.tensor_scalar(pick[:, TT + a:TT + b, :], ci[:, a:b, :], 15, None, ALU.bitwise_and))
                link(v.tensor_copy(of(pos_f), of(pick)))
                shape = [P, b - a, TOPK, TOPK]
                at = [(q * TT + a, q * TT + b) for q in range(2)]
                link(*[v.tensor_tensor(hot[:, i:j, :, :], pos_f[:, i:j, :].unsqueeze(3).to_broadcast(shape),
                                       C("iota").unsqueeze(1).unsqueeze(1).to_broadcast(shape), ALU.is_equal) for i, j in at])
                link(*[v.tensor_tensor(hot[:, i:j, :, :], hot[:, i:j, :, :], side[:, i:j, :].unsqueeze(2).to_broadcast(shape),
                                       ALU.mult) for i, j in at])
                link(*[v.tensor_reduce(side_no[:, i:j, :], hot[:, i:j, :, :], AX_X, ALU.add) for i, j in at])
                v.scalar_tensor_tensor(out=idx[:, stage % 2, a:b, h * TOPK:(h + 1) * TOPK], in0=side_no[:, a:b, :],
                                       scalar=float(PK), in1=side_no[:, TT + a:TT + b, :], op0=ALU.mult, op1=ALU.add)\
                    .then_inc(idx_ready, b - a)

            def search(stage, h):
                k = n.up("scores")
                dve.wait_ge(*taken["scores", k])
                for tiles in ([[0], [1]] if h == 0 else [[0, 1]]):
                    find(stage, h, tiles)
                    n.up("exp")
                dve.wait_ge(exp_ready, n["exp"])
                link(v.tensor_reduce(e_stat[:, 0, :], e16[:, :, :], AX_X, ALU.add))
                link(v.reciprocal(e_stat[:, 1, :], e_stat[:, 0, :]))
                v.tensor_tensor(gw[:, stage % 2, :, h * TOPK:(h + 1) * TOPK], e16[:, :, :],
                                e_stat[:, 1, :].unsqueeze(2).to_broadcast([P, TT, TOPK]), ALU.mult).then_inc(sc_used, 1)
                dve.wait_ge(sc_used, k)

            steps = {"ada": ada_pair, "mods": mods, "gate": gate, "rms": rms, "norm": norm, "norm_ctx": norm_ctx, "v_norm": v_norm,
                     "ac_cols": ac_cols, "spatial": spatial, "ab_cols": ab_cols, "lam": lam, "ca_cols": ca_cols,
                     "conv": conv, "kc_norm": kc_norm, "qk_norm": qk_norm, "attend": attend, "conv_norm": conv_norm,
                     "o_norm": o_norm, "out_rows": out_rows, "out_half": out_half, "search": search}

            def dots_and_weights(T, it):
                stage, t = T // TT, T % TT

                def dot(c):
                    s = c % RING
                    dve.wait_ge(uv_landed[s], it * 16 + 16 * (T * NBODY + 1))
                    v.tensor_tensor_reduce(out=uv[:, s, 0:D], in0=uv[:, s, 0:D], in1=h2[:, stage % 2, t, :], scale=1.0, scalar=0.0,
                                           op0=ALU.mult, op1=ALU.add, accum_out=dots[:, c:c + 1]).then_inc(dots_ready, 1)

                def weigh(c):
                    s = c % RING
                    dve.wait_ge(gelu_ready, it * BODY + (T * NSEL + c + 1))
                    dve.wait_ge(uv_used, it * BODY + (T * NSEL + c + 1))
                    v.tensor_scalar(diag[:, s, :], C("ident"), gel[:, c:c + 1], gw[:, stage % 2, t, bass.ds(it * BODY + c, 1)],
                                    ALU.mult, ALU.mult).then_inc(diag_ready, 1)

                for c in range(BODY):
                    dot(c)
                    if c:
                        weigh(c - 1)
                weigh(BODY - 1)

            def bodies(T, first, count):
                if count == 1:
                    dots_and_weights(T, first)
                    return
                with dve.Fori(first, first + count) as it:
                    dots_and_weights(T, it)

            def open_tile(T):
                stage, t = T // TT, T % TT
                dve.wait_ge(*taken["h2", stage, t])

            def close_tile(T):
                stage, t = T // TT, T % TT
                dve.wait_ge(acc_ready, T + 1)
                dve.wait_ge(*taken["gate", stage, 1])
                tmp = h2[:, stage % 2, t, :]
                v.tensor_tensor(tmp, acc.rearrange("p a b -> p (a b)"), gate_peer[:, stage % 2, :], ALU.mult).then_inc(acc_free, 1)
                dve.wait_ge(acc_free, T + 1)
                row = x[:, tile_of(stage, t), :]
                done = v.tensor_tensor(row, row, tmp, ALU.add)
                if stage == 2:
                    done.then_inc(x_rows_ready, 1)
                else:
                    link(done)

            v.memset(ones[:, :], 1.0).then_inc(constants_set, 1)
            v.memset(zeros[:, :], 0.0).then_inc(constants_set, 1)
            dve.wait_ge(const_loaded, 16)
            walk(steps, open_tile, bodies, close_tile)


def in_columns(w):
    k, n = w.shape
    return w.reshape(k // P, P, n // BLK, BLK).transpose(2, 1, 0, 3).reshape(n // BLK, P, k // P * BLK)


def columns(a):
    a = a.reshape(-1, a.shape[-1] // P, P)
    return a.transpose(2, 0, 1).reshape(P, -1)


def rows_(a):
    return np.broadcast_to(a.reshape(1, -1), (P, a.size))


def kernel(x, c, ctx, c_ctx, w_ada, b_ada, norm1_g, norm2_g, w_in, w_out, a_conv_w, b_vnorm_g, b_spatial_w, b_spatial_b,
           c_conv_w, c_conv_b, c_norm_g, d_qk_norm_g, d_lambda, d_subln_g, peer_wq, peer_subkeys, peer_u, peer_v):
    import concourse.bacc as bacc
    from concourse.bass_utils import run_bass_kernel_spmd

    f = lambda a: np.asarray(a)
    x, c, ctx, c_ctx, w_ada, w_in, w_out, peer_wq = map(f, (x, c, ctx, c_ctx, w_ada, w_in, w_out, peer_wq))
    ts = f(b_spatial_w)[0].transpose(2, 0, 1)
    tok = np.arange(TOK)
    inv = (10000.0 ** (-np.arange(16, dtype=np.float32) / 16)).astype(np.float32)
    ang = np.concatenate([(tok // GRID_W).astype(np.float32)[:, None] * inv, (tok % GRID_W).astype(np.float32)[:, None] * inv], -1)
    table = lambda a: a.astype(np.float32).reshape(TT, P, 32).transpose(1, 0, 2).reshape(P, -1)
    part = {
        "ident": np.eye(P, dtype=np.float32),
        "iota": rows_(np.arange(TOPK, dtype=np.float32)),
        "cos": table(np.cos(ang)), "sin": table(np.sin(ang)),
        "c": np.stack([c[0], c_ctx], -1).reshape(KC, P, 2).transpose(1, 0, 2).reshape(P, -1),
        "b_ada": columns(f(b_ada)),
        "norm_g": columns(np.stack([f(norm1_g), f(norm2_g)], 1)),
        "a_conv": f(a_conv_w)[0].reshape(CONV_A, MC, P).transpose(2, 1, 0).reshape(P, -1),
        "c_conv": f(c_conv_w)[0].reshape(CONV_C, MC, P).transpose(2, 1, 0).reshape(P, -1),
        "c_conv_b": columns(f(c_conv_b)), "c_norm_g": columns(f(c_norm_g)),
        "vnorm_g": rows_(f(b_vnorm_g)), "qk_g": rows_(f(d_qk_norm_g)), "subln_g": rows_(f(d_subln_g)),
        "lam": rows_(f(d_lambda)),
        "b_spatial": np.repeat(f(b_spatial_b)[0].reshape(MC, 2, P).transpose(1, 0, 2), P // 2, axis=0).reshape(P, -1),
    }
    const = np.concatenate([part[name] for name, _ in PARTS], 1)
    wq = []
    for layer in range(2):
        keys = f(peer_subkeys)[layer].transpose(0, 3, 1, 2).reshape(PH, P, 2 * PK)
        wq.append(np.concatenate([in_columns(peer_wq[layer]), keys], 2))
    arrays = {
        "const": np.ascontiguousarray(const),
        "wst": np.ascontiguousarray(ts.transpose(0, 1, 2).reshape(P, -1)),
        "xin": np.concatenate([ctx[0].reshape(TT, P, D), x[0].reshape(TT, P, D)], 0),
        "ada": np.stack([in_columns(w_ada[i]) for i in range(2)]),
        "in": np.stack([in_columns(w_in[i]) for i in range(2)]),
        "out_w": in_columns(w_out[0])[None],
        "out2": w_out[1].reshape(2, MC, P, 2, 512).transpose(0, 3, 2, 1, 4).reshape(1, 4, P, BLK_W),
        "wq": np.stack(wq),
        "uv0": np.concatenate([f(peer_u)[0], f(peer_v)[0]], 1),
        "uv1": np.concatenate([f(peer_u)[1], f(peer_v)[1]], 1),
    }
    nc = bacc.Bacc("TRN2", target_bir_lowering=False, num_devices=1)
    A = {name: nc.dram_tensor(name + "_dram", a.shape, F32, kind="ExternalInput").ap() for name, a in arrays.items()}
    out = nc.dram_tensor("out_dram", (TT, P, D), F32, kind="ExternalOutput").ap()
    A["result"] = out
    build(nc, A)
    r = run_bass_kernel_spmd(nc, [{name + "_dram": a for name, a in arrays.items()}], core_ids=[0])
    return r.results[0]["out_dram"].reshape(1, TOK, D)
```
